# Optimizing a Trainium2 kernel written in Bass

```python
import math
import jax, jax.numpy as jnp
from jax import lax
import numpy as np

D_MODEL = 1024
BATCH = 1
SEQ = 512
DEPTH = 2

N_MIXERS = 2
N_CONV = (DEPTH + 1) // 2
N_ATTN = DEPTH // 2
CONV_WIDTH = 31
N_HEADS = 8
HEAD_DIM = D_MODEL // (2 * N_HEADS)
V_DIM = 2 * HEAD_DIM
Q_BLOCK = 128
NUM_BUCKETS = 32
MAX_EXACT = NUM_BUCKETS // 2
MAX_DISTANCE = 128
D_FF = int(math.ceil(8 * D_MODEL / 3 / 256) * 256)
PLE_DIM = 256
EPS = 1e-6


def rms_norm(x, g):
    xf = x.astype(jnp.float32)
    y = xf * lax.rsqrt(jnp.mean(xf * xf, axis=-1, keepdims=True) + EPS)
    return (y * g.astype(jnp.float32)).astype(x.dtype)

def layer_norm(x, g, b):
    xf = x.astype(jnp.float32)
    mu = jnp.mean(xf, axis=-1, keepdims=True)
    xc = xf - mu
    var = jnp.mean(xc * xc, axis=-1, keepdims=True)
    y = xc * lax.rsqrt(var + EPS) * g.astype(jnp.float32) + b.astype(jnp.float32)
    return y.astype(x.dtype)

def conformer_conv(x, w_pw1, b_pw1, dw_w, dw_b, ln_g, ln_b, w_pw2, b_pw2):
    a = x @ w_pw1 + b_pw1
    u = a[..., :D_MODEL] * jax.nn.sigmoid(a[..., D_MODEL:])
    u = lax.conv_general_dilated(
        u, dw_w[:, None, :].astype(u.dtype), window_strides=(1,),
        padding=[(CONV_WIDTH - 1, 0)],
        dimension_numbers=("NWC", "WIO", "NWC"),
        feature_group_count=D_MODEL) + dw_b
    u = jax.nn.silu(layer_norm(u, ln_g, ln_b))
    return u @ w_pw2 + b_pw2

def t5_bucket(dist):
    n = jnp.maximum(dist, 0)
    is_small = n < MAX_EXACT
    nf = jnp.maximum(n, 1).astype(jnp.float32)
    large = MAX_EXACT + (jnp.log(nf / MAX_EXACT) / math.log(MAX_DISTANCE / MAX_EXACT)
                         * (NUM_BUCKETS - MAX_EXACT)).astype(jnp.int32)
    large = jnp.minimum(large, NUM_BUCKETS - 1)
    return jnp.where(is_small, n, large)

def diff_attention(x, w_qkv, q_g, k_g, lq1, lk1, lq2, lk2, sub_g, w_o, rel_bias, lambda_init):
    B, S, _ = x.shape
    qkv = x @ w_qkv
    q, k, v = jnp.split(qkv, 3, axis=-1)
    q = rms_norm(q.reshape(B, S, N_HEADS, 2, HEAD_DIM), q_g) * (HEAD_DIM ** -0.5)
    k = rms_norm(k.reshape(B, S, N_HEADS, 2, HEAD_DIM), k_g)
    v = v.reshape(B, S, N_HEADS, V_DIM)
    q = jnp.transpose(q, (0, 2, 3, 1, 4))
    k = jnp.transpose(k, (0, 2, 3, 1, 4))
    v = jnp.transpose(v, (0, 2, 1, 3))
    lam = (jnp.exp(jnp.sum(lq1.astype(jnp.float32) * lk1.astype(jnp.float32)))
           - jnp.exp(jnp.sum(lq2.astype(jnp.float32) * lk2.astype(jnp.float32)))
           + lambda_init)
    n_blk = S // Q_BLOCK
    qb = jnp.moveaxis(q.reshape(B, N_HEADS, 2, n_blk, Q_BLOCK, HEAD_DIM), 3, 0)
    k_pos = jnp.arange(S, dtype=jnp.int32)

    def block(args):
        q_blk, bi = args
        q_pos = bi * Q_BLOCK + jnp.arange(Q_BLOCK, dtype=jnp.int32)
        dist = q_pos[:, None] - k_pos[None, :]
        bias = jnp.transpose(rel_bias[t5_bucket(dist)], (2, 0, 1)).astype(jnp.float32)
        logits = jnp.einsum('bhcqd,bhckd->bhcqk', q_blk, k).astype(jnp.float32)
        logits = logits + bias[None, :, None]
        logits = jnp.where(dist >= 0, logits, -jnp.inf)
        probs = jax.nn.softmax(logits, axis=-1)
        w = probs[:, :, 0] - lam * probs[:, :, 1]
        return jnp.einsum('bhqk,bhkd->bhqd', w.astype(v.dtype), v)

    outs = lax.map(block, (qb, jnp.arange(n_blk, dtype=jnp.int32)))
    o = jnp.transpose(outs, (1, 0, 3, 2, 4)).reshape(B, S, N_HEADS, V_DIM)
    o = rms_norm(o, sub_g) * (1.0 - lambda_init)
    return o.reshape(B, S, N_HEADS * V_DIM) @ w_o

def swiglu(x, w_gate, w_up, w_down):
    return (jax.nn.silu(x @ w_gate) * (x @ w_up)) @ w_down

def first_inputs(seed: int = 0) -> dict:
    key = jax.random.key(seed)
    ks = iter(jax.random.split(key, 64))
    f32 = jnp.float32

    def nrm(shape, scale):
        return jax.random.normal(next(ks), shape, f32) * scale

    def gain(shape):
        return 1.0 + nrm(shape, 0.05)

    D = D_MODEL
    return {
        "x": nrm((BATCH, SEQ, D), 1.0),
        "p": nrm((DEPTH, BATCH, SEQ, PLE_DIM), 1.0),
        "conv_norm_g": gain((N_CONV, D)),
        "conv_w_pw1": nrm((N_CONV, D, 2 * D), D ** -0.5),
        "conv_b_pw1": nrm((N_CONV, 2 * D), 0.02),
        "conv_dw_w": nrm((N_CONV, CONV_WIDTH, D), CONV_WIDTH ** -0.5),
        "conv_dw_b": nrm((N_CONV, D), 0.02),
        "conv_ln_g": gain((N_CONV, D)),
        "conv_ln_b": nrm((N_CONV, D), 0.02),
        "conv_w_pw2": nrm((N_CONV, D, D), D ** -0.5),
        "conv_b_pw2": nrm((N_CONV, D), 0.02),
        "attn_norm_g": gain((N_ATTN, D)),
        "attn_w_qkv": nrm((N_ATTN, D, 3 * D), D ** -0.5),
        "attn_q_norm_g": gain((N_ATTN, HEAD_DIM)),
        "attn_k_norm_g": gain((N_ATTN, HEAD_DIM)),
        "attn_lambda_q1": nrm((N_ATTN, HEAD_DIM), 0.1),
        "attn_lambda_k1": nrm((N_ATTN, HEAD_DIM), 0.1),
        "attn_lambda_q2": nrm((N_ATTN, HEAD_DIM), 0.1),
        "attn_lambda_k2": nrm((N_ATTN, HEAD_DIM), 0.1),
        "attn_sub_norm_g": gain((N_ATTN, V_DIM)),
        "attn_w_o": nrm((N_ATTN, D, D), D ** -0.5),
        "rel_bias": nrm((NUM_BUCKETS, N_HEADS), 0.5),
        "ffn_norm_g": gain((DEPTH, D)),
        "ffn_w_gate": nrm((DEPTH, D, D_FF), D ** -0.5),
        "ffn_w_up": nrm((DEPTH, D, D_FF), D ** -0.5),
        "ffn_w_down": nrm((DEPTH, D_FF, D), D_FF ** -0.5),
        "ple_norm_g": gain((DEPTH, D)),
        "ple_w_gate": nrm((DEPTH, D, D), D ** -0.5),
        "ple_w_proj": nrm((DEPTH, PLE_DIM, D), PLE_DIM ** -0.5),
    }

def first_block(x, p, conv_norm_g, conv_w_pw1, conv_b_pw1, conv_dw_w, conv_dw_b, conv_ln_g,
              conv_ln_b, conv_w_pw2, conv_b_pw2, attn_norm_g, attn_w_qkv, attn_q_norm_g,
              attn_k_norm_g, attn_lambda_q1, attn_lambda_k1, attn_lambda_q2, attn_lambda_k2,
              attn_sub_norm_g, attn_w_o, rel_bias, ffn_norm_g, ffn_w_gate, ffn_w_up, ffn_w_down,
              ple_norm_g, ple_w_gate, ple_w_proj):
    h = x
    for i in range(DEPTH):
        j = i // N_MIXERS
        if i % N_MIXERS == 0:
            u = rms_norm(h, conv_norm_g[j])
            h = h + conformer_conv(u, conv_w_pw1[j], conv_b_pw1[j], conv_dw_w[j], conv_dw_b[j],
                                   conv_ln_g[j], conv_ln_b[j], conv_w_pw2[j], conv_b_pw2[j])
        else:
            lambda_init = 0.8 - 0.6 * math.exp(-0.3 * i)
            u = rms_norm(h, attn_norm_g[j])
            h = h + diff_attention(u, attn_w_qkv[j], attn_q_norm_g[j], attn_k_norm_g[j],
                                   attn_lambda_q1[j], attn_lambda_k1[j], attn_lambda_q2[j],
                                   attn_lambda_k2[j], attn_sub_norm_g[j], attn_w_o[j],
                                   rel_bias, lambda_init)
        u = rms_norm(h, ffn_norm_g[i])
        h = h + swiglu(u, ffn_w_gate[i], ffn_w_up[i], ffn_w_down[i])
        gate = jax.nn.sigmoid(rms_norm(h, ple_norm_g[i]) @ ple_w_gate[i])
        h = h + gate * (p[i] @ ple_w_proj[i])
    return h


CHUNK = 64
A_HEADS = 8
A_HEAD_DIM = 64
A_WIDTH = A_HEADS * A_HEAD_DIM
IDX_HEADS = 8
IDX_DIM = 64
TOPK_MAX = 256
B_WIDTH = 512
B_GROUPS = 8
SHORT_CONV = 3
C_WIDTH = 512
POOL_WINDOWS = (2, 4, 8, 16)
C_GROUPS = len(POOL_WINDOWS)
C_GROUP_DIM = C_WIDTH // C_GROUPS
D_HEADS = 8
D_NOPE = 64
D_ROPE = 32
D_V = 64
Q_LORA = 384
KV_LORA = 256
ROPE_BASE = 10000.0
D_FF_2 = 2816
FFN_CONV = 3
LN_EPS = 1e-5
RMS_EPS = 1e-6
DN_ALPHA = (2 * DEPTH) ** 0.25
DN_BETA = (8 * DEPTH) ** -0.25
NEG = -1e30

EVEN_SIZES = (A_WIDTH, A_WIDTH, A_WIDTH, IDX_HEADS * IDX_DIM, IDX_DIM, IDX_HEADS,
              B_WIDTH, B_WIDTH, B_WIDTH)
EVEN_IN = sum(EVEN_SIZES)
EVEN_OUT = A_WIDTH + B_WIDTH
ODD_SIZES = (C_WIDTH, Q_LORA, KV_LORA, D_ROPE)
ODD_IN = sum(ODD_SIZES)
ODD_OUT = C_WIDTH + D_HEADS * D_V
N_EVEN = (DEPTH + 1) // 2
N_ODD = DEPTH // 2


def _split(z, sizes):
    offs = []
    acc = 0
    for s in sizes[:-1]:
        acc += s
        offs.append(acc)
    return jnp.split(z, offs, axis=-1)

def layer_norm_2(x, g, b):
    x32 = x.astype(jnp.float32)
    mu = jnp.mean(x32, axis=-1, keepdims=True)
    var = jnp.mean(jnp.square(x32 - mu), axis=-1, keepdims=True)
    y = (x32 - mu) * lax.rsqrt(var + LN_EPS)
    return (y * g.astype(jnp.float32) + b.astype(jnp.float32)).astype(x.dtype)

def rms_norm_2(x, g):
    x32 = x.astype(jnp.float32)
    y = x32 * lax.rsqrt(jnp.mean(jnp.square(x32), axis=-1, keepdims=True) + RMS_EPS)
    return (y * g.astype(jnp.float32)).astype(x.dtype)

def causal_dwconv(x, w):
    k_w = w.shape[0]
    seq = x.shape[1]
    xp = jnp.pad(x, ((0, 0), (k_w - 1, 0), (0, 0)))
    y = xp[:, 0:seq] * w[0]
    for k in range(1, k_w):
        y = y + xp[:, k:k + seq] * w[k]
    return y

def chunk_limit(pos):
    return (pos // CHUNK + 1) * CHUNK

def alibi_slopes(n):
    return jnp.asarray([2.0 ** (-8.0 * (i + 1) / n) for i in range(n)], dtype=jnp.float32)

def rope_tables(seq, dim):
    inv = ROPE_BASE ** (-jnp.arange(0, dim, 2, dtype=jnp.float32) / dim)
    ang = jnp.arange(seq, dtype=jnp.float32)[:, None] * inv[None, :]
    return jnp.cos(ang), jnp.sin(ang)

def apply_rope(x, cos, sin):
    half = x.shape[-1] // 2
    x1, x2 = x[..., :half], x[..., half:]
    c = cos[None, :, None, :].astype(x.dtype)
    s = sin[None, :, None, :].astype(x.dtype)
    return jnp.concatenate([x1 * c - x2 * s, x2 * c + x1 * s], axis=-1)

def dsa_attention(q, k, v, q_idx, k_idx, w_idx):
    bsz, seq = q.shape[0], q.shape[1]
    topk = min(TOPK_MAX, seq // 4)
    nblk = seq // Q_BLOCK
    key_pos = jnp.arange(seq)
    slopes = alibi_slopes(A_HEADS)
    w_scaled = w_idx * (IDX_HEADS ** -0.5 * IDX_DIM ** -0.5)
    scale = A_HEAD_DIM ** -0.5

    def block(i):
        start = i * Q_BLOCK
        qb = lax.dynamic_slice_in_dim(q, start, Q_BLOCK, axis=1)
        qib = lax.dynamic_slice_in_dim(q_idx, start, Q_BLOCK, axis=1)
        wb = lax.dynamic_slice_in_dim(w_scaled, start, Q_BLOCK, axis=1)
        qpos = start + jnp.arange(Q_BLOCK)
        limit = chunk_limit(qpos)
        rel = jax.nn.relu(jnp.einsum('bthd,bsd->bths', qib, k_idx))
        score = jnp.einsum('bths,bth->bts', rel, wb)
        admissible = key_pos[None, :] < limit[:, None]
        score = jnp.where(admissible[None], score, NEG)
        _, idx = lax.top_k(score, topk)
        valid = idx < limit[None, :, None]
        k_sel = jax.vmap(lambda kk, ii: kk[ii])(k, idx)
        v_sel = jax.vmap(lambda vv, ii: vv[ii])(v, idx)
        logits = jnp.einsum('bthd,btjhd->bthj', qb, k_sel).astype(jnp.float32) * scale
        dist = jnp.abs(qpos[None, :, None] - idx).astype(jnp.float32)
        logits = logits - slopes[None, None, :, None] * dist[:, :, None, :]
        logits = jnp.where(valid[:, :, None, :], logits, NEG)
        p = jax.nn.softmax(logits, axis=-1).astype(v.dtype)
        return jnp.einsum('bthj,btjhd->bthd', p, v_sel)

    out = lax.map(block, jnp.arange(nblk))
    return jnp.moveaxis(out, 0, 1).reshape(bsz, seq, A_WIDTH)

def multiscale_pool(u, pool_w, pool_scale):
    bsz, seq = u.shape[0], u.shape[1]
    ug = u.reshape(bsz, seq, C_GROUPS, C_GROUP_DIM)
    cs = jnp.cumsum(ug.astype(jnp.float32), axis=1)
    cs = jnp.pad(cs, ((0, 0), (1, 0), (0, 0), (0, 0)))
    pos = jnp.arange(seq)
    means = []
    for g, win in enumerate(POOL_WINDOWS):
        hi = cs[:, 1:, g]
        lo = cs[:, jnp.maximum(pos + 1 - win, 0), g]
        cnt = jnp.minimum(pos + 1, win).astype(jnp.float32)
        means.append((hi - lo) / cnt[None, :, None])
    pooled = jnp.stack(means, axis=2).astype(u.dtype) - ug
    mixed = jnp.einsum('bsgc,gcd->bsgd', pooled, pool_w)
    return mixed.reshape(bsz, seq, C_WIDTH) * pool_scale

def mla_attention(q_lat, kv_lat, k_rope_in, q_norm_g, w_uq, kv_norm_g, w_ukv):
    bsz, seq = q_lat.shape[0], q_lat.shape[1]
    q = (rms_norm_2(q_lat, q_norm_g) @ w_uq).reshape(bsz, seq, D_HEADS, D_NOPE + D_ROPE)
    q_nope, q_rope = q[..., :D_NOPE], q[..., D_NOPE:]
    kv = (rms_norm_2(kv_lat, kv_norm_g) @ w_ukv).reshape(bsz, seq, D_HEADS, D_NOPE + D_V)
    k_nope, v = kv[..., :D_NOPE], kv[..., D_NOPE:]
    cos, sin = rope_tables(seq, D_ROPE)
    q_rope = apply_rope(q_rope, cos, sin)
    k_rope = apply_rope(k_rope_in[:, :, None, :], cos, sin)
    qh = jnp.concatenate([q_nope, q_rope], axis=-1)
    kh = jnp.concatenate([k_nope, jnp.broadcast_to(k_rope, (bsz, seq, D_HEADS, D_ROPE))], axis=-1)
    scale = (D_NOPE + D_ROPE) ** -0.5
    key_pos = jnp.arange(seq)
    nblk = seq // Q_BLOCK

    def block(i):
        start = i * Q_BLOCK
        qb = lax.dynamic_slice_in_dim(qh, start, Q_BLOCK, axis=1)
        limit = chunk_limit(start + jnp.arange(Q_BLOCK))
        logits = jnp.einsum('bthd,bshd->bhts', qb, kh).astype(jnp.float32) * scale
        mask = key_pos[None, :] < limit[:, None]
        logits = jnp.where(mask[None, None], logits, NEG)
        p = jax.nn.softmax(logits, axis=-1).astype(v.dtype)
        return jnp.einsum('bhts,bshd->bthd', p, v)

    out = lax.map(block, jnp.arange(nblk))
    return jnp.moveaxis(out, 0, 1).reshape(bsz, seq, D_HEADS * D_V)

def even_mixer(h, w_in, conv_w, w_out):
    bsz, seq = h.shape[0], h.shape[1]
    z = h @ w_in
    q, k, v, qi, ki, wi, bg, cg, xb = _split(z, EVEN_SIZES)
    ya = dsa_attention(q.reshape(bsz, seq, A_HEADS, A_HEAD_DIM),
                       k.reshape(bsz, seq, A_HEADS, A_HEAD_DIM),
                       v.reshape(bsz, seq, A_HEADS, A_HEAD_DIM),
                       qi.reshape(bsz, seq, IDX_HEADS, IDX_DIM), ki, wi)
    yb = bg * causal_dwconv(cg * xb, conv_w)
    return jnp.concatenate([ya, yb], axis=-1) @ w_out

def odd_mixer(h, w_in, pool_w, pool_scale, q_norm_g, w_uq, kv_norm_g, w_ukv, w_out):
    z = h @ w_in
    u, q_lat, kv_lat, k_rope = _split(z, ODD_SIZES)
    yc = multiscale_pool(u, pool_w, pool_scale)
    yd = mla_attention(q_lat, kv_lat, k_rope, q_norm_g, w_uq, kv_norm_g, w_ukv)
    return jnp.concatenate([yc, yd], axis=-1) @ w_out

def conv_ffn(h, w_up, conv_w, w_down):
    u = causal_dwconv(h @ w_up, conv_w)
    val, gate = u[..., :D_FF_2], u[..., D_FF_2:]
    return (jax.nn.silu(gate) * val) @ w_down

def second_inputs(seed: int = 0) -> dict:
    key = jax.random.key(seed)
    ks = iter(jax.random.split(key, 40))
    f32 = jnp.float32

    def nrm(shape, scale):
        return jax.random.normal(next(ks), shape, f32) * scale

    d = D_MODEL
    x = nrm((BATCH, SEQ, d), 1.0)
    c = nrm((BATCH, d), 1.0)
    ada_w = nrm((DEPTH, d, 6 * d), 0.1 * d ** -0.5)
    ada_b = nrm((DEPTH, 6 * d), 0.01)
    ln_mix_g = 1.0 + nrm((DEPTH, d), 0.01)
    ln_mix_b = nrm((DEPTH, d), 0.01)
    ln_ffn_g = 1.0 + nrm((DEPTH, d), 0.01)
    ln_ffn_b = nrm((DEPTH, d), 0.01)

    even_col_scale = jnp.concatenate([
        jnp.ones((2 * A_WIDTH,), f32), jnp.full((A_WIDTH,), DN_BETA, f32),
        jnp.ones((EVEN_IN - 3 * A_WIDTH,), f32)])
    ev_w_in = nrm((N_EVEN, d, EVEN_IN), d ** -0.5) * even_col_scale
    ev_conv_w = nrm((N_EVEN, SHORT_CONV, B_WIDTH), SHORT_CONV ** -0.5)
    ev_w_out = nrm((N_EVEN, EVEN_OUT, d), DN_BETA * EVEN_OUT ** -0.5)

    od_w_in = nrm((N_ODD, d, ODD_IN), d ** -0.5)
    pool_w = nrm((N_ODD, C_GROUPS, C_GROUP_DIM, C_GROUP_DIM), C_GROUP_DIM ** -0.5)
    pool_scale = 1.0 + nrm((N_ODD, C_WIDTH), 0.1)
    q_norm_g = 1.0 + nrm((N_ODD, Q_LORA), 0.01)
    w_uq = nrm((N_ODD, Q_LORA, D_HEADS * (D_NOPE + D_ROPE)), Q_LORA ** -0.5)
    kv_norm_g = 1.0 + nrm((N_ODD, KV_LORA), 0.01)
    ukv_col_scale = jnp.tile(jnp.concatenate([jnp.ones((D_NOPE,), f32),
                                              jnp.full((D_V,), DN_BETA, f32)]), D_HEADS)
    w_ukv = nrm((N_ODD, KV_LORA, D_HEADS * (D_NOPE + D_V)), KV_LORA ** -0.5) * ukv_col_scale
    od_w_out = nrm((N_ODD, ODD_OUT, d), DN_BETA * ODD_OUT ** -0.5)

    ffn_w_up = nrm((DEPTH, d, 2 * D_FF_2), d ** -0.5)
    ffn_conv_w = nrm((DEPTH, FFN_CONV, 2 * D_FF_2), FFN_CONV ** -0.5)
    ffn_w_down = nrm((DEPTH, D_FF_2, d), DN_BETA * D_FF_2 ** -0.5)

    return {"x": x, "c": c, "ada_w": ada_w, "ada_b": ada_b,
            "ln_mix_g": ln_mix_g, "ln_mix_b": ln_mix_b, "ln_ffn_g": ln_ffn_g, "ln_ffn_b": ln_ffn_b,
            "ev_w_in": ev_w_in, "ev_conv_w": ev_conv_w, "ev_w_out": ev_w_out,
            "od_w_in": od_w_in, "pool_w": pool_w, "pool_scale": pool_scale,
            "q_norm_g": q_norm_g, "w_uq": w_uq, "kv_norm_g": kv_norm_g, "w_ukv": w_ukv,
            "od_w_out": od_w_out,
            "ffn_w_up": ffn_w_up, "ffn_conv_w": ffn_conv_w, "ffn_w_down": ffn_w_down}

def second_block(x, c, ada_w, ada_b, ln_mix_g, ln_mix_b, ln_ffn_g, ln_ffn_b,
              ev_w_in, ev_conv_w, ev_w_out,
              od_w_in, pool_w, pool_scale, q_norm_g, w_uq, kv_norm_g, w_ukv, od_w_out,
              ffn_w_up, ffn_conv_w, ffn_w_down):
    cond = jax.nn.silu(c)
    for l in range(DEPTH):
        mod = (cond @ ada_w[l] + ada_b[l])[:, None, :]
        sh_m, sc_m, g_m, sh_f, sc_f, g_f = jnp.split(mod, 6, axis=-1)
        h = x * (1.0 + sc_m) + sh_m
        if l % 2 == 0:
            e = l // 2
            y = even_mixer(h, ev_w_in[e], ev_conv_w[e], ev_w_out[e])
        else:
            o = l // 2
            y = odd_mixer(h, od_w_in[o], pool_w[o], pool_scale[o], q_norm_g[o], w_uq[o],
                          kv_norm_g[o], w_ukv[o], od_w_out[o])
        x = layer_norm_2(DN_ALPHA * x + (1.0 + g_m) * y, ln_mix_g[l], ln_mix_b[l])
        h = x * (1.0 + sc_f) + sh_f
        y = conv_ffn(h, ffn_w_up[l], ffn_conv_w[l], ffn_w_down[l])
        x = layer_norm_2(DN_ALPHA * x + (1.0 + g_f) * y, ln_ffn_g[l], ln_ffn_b[l])
    return x


def setup_inputs(seed=0):
    out = dict(first_inputs(seed))
    for name, value in second_inputs(seed + 1).items():
        if name != "x":
            out[name + "_2"] = value
    return out


def reference(
    x, p, conv_norm_g, conv_w_pw1, conv_b_pw1, conv_dw_w, conv_dw_b, conv_ln_g, conv_ln_b,
    conv_w_pw2, conv_b_pw2, attn_norm_g, attn_w_qkv, attn_q_norm_g, attn_k_norm_g,
    attn_lambda_q1, attn_lambda_k1, attn_lambda_q2, attn_lambda_k2, attn_sub_norm_g, attn_w_o,
    rel_bias, ffn_norm_g, ffn_w_gate, ffn_w_up, ffn_w_down, ple_norm_g, ple_w_gate, ple_w_proj,
    c_2, ada_w_2, ada_b_2, ln_mix_g_2, ln_mix_b_2, ln_ffn_g_2, ln_ffn_b_2, ev_w_in_2,
    ev_conv_w_2, ev_w_out_2, od_w_in_2, pool_w_2, pool_scale_2, q_norm_g_2, w_uq_2, kv_norm_g_2,
    w_ukv_2, od_w_out_2, ffn_w_up_2, ffn_conv_w_2, ffn_w_down_2,
):
    x = first_block(
        x, p, conv_norm_g, conv_w_pw1, conv_b_pw1, conv_dw_w, conv_dw_b, conv_ln_g, conv_ln_b,
        conv_w_pw2, conv_b_pw2, attn_norm_g, attn_w_qkv, attn_q_norm_g, attn_k_norm_g,
        attn_lambda_q1, attn_lambda_k1, attn_lambda_q2, attn_lambda_k2, attn_sub_norm_g,
        attn_w_o, rel_bias, ffn_norm_g, ffn_w_gate, ffn_w_up, ffn_w_down, ple_norm_g,
        ple_w_gate, ple_w_proj,
    )
    return second_block(
        x, c_2, ada_w_2, ada_b_2, ln_mix_g_2, ln_mix_b_2, ln_ffn_g_2, ln_ffn_b_2, ev_w_in_2,
        ev_conv_w_2, ev_w_out_2, od_w_in_2, pool_w_2, pool_scale_2, q_norm_g_2, w_uq_2,
        kv_norm_g_2, w_ukv_2, od_w_out_2, ffn_w_up_2, ffn_conv_w_2, ffn_w_down_2,
    )


_drawn_inputs = setup_inputs


def setup_inputs(seed=0):
    import zlib

    import numpy as np

    out = dict(_drawn_inputs(seed))
    spreads = {}
    factors = {'attn_lambda_k2': 2.992,
     'ple_norm_g': 3.713,
     'ada_b_2': 3.18,
     'ln_mix_g_2': 3.728,
     'ln_mix_b_2': 3.979,
     'ln_ffn_g_2': 3.982,
     'ln_ffn_b_2': 4.013,
     'q_norm_g_2': 8.0,
     'w_uq_2': 4.317,
     'kv_norm_g_2': 8.0}
    for name, (base, spread) in spreads.items():
        noise = np.random.default_rng([zlib.crc32(name.encode()), seed]).standard_normal(out[name].shape)
        drawn = base * np.exp(spread * noise) if base else spread * noise
        out[name] = __import__('jax').numpy.asarray(drawn.astype(out[name].dtype))
    for name, factor in factors.items():
        out[name] = (out[name] * factor).astype(out[name].dtype)
    return out
```

```python
import math
from contextlib import ExitStack

import concourse.bass as bass
import numpy as np
from concourse import mybir

F32 = mybir.dt.float32
ALU = mybir.AluOpType
ACT = mybir.ActivationFunctionType
AX = mybir.AxisListType

P = 128
S = 512
D = 1024
DC = D // P
NB = S // P
FF = 2816
FC = FF // P
CONV = 31
PLE = 256
HEADS = 8
LAMBDA_INIT = 0.8 - 0.6 * math.exp(-0.3)
BUCKETS = 32
DN_ALPHA = 4 ** 0.25
EPS_RMS, EPS_LN = 1e-6, 1e-5
NEG = -1e30
TAKEN = -3e38
TOPK = 128
QL, KVL, ROPE, NOPE = 384, 256, 32, 64
QK_DIM = NOPE + ROPE
WINDOWS = (2, 4, 8, 16)
RING = 4
BANKS = 4
SLOT = 2048

PARAM_WIDTHS = [
    ("conv_norm_g", 8), ("conv_b_pw1", 16), ("conv_dw_w", 8 * CONV), ("conv_dw_b", 8),
    ("conv_ln_g", 8), ("conv_ln_b", 8), ("conv_b_pw2", 8), ("attn_norm_g", 8),
    ("q_norm_g", 1), ("k_norm_g", 1), ("sub_norm_g", 1), ("lambda", 4),
    ("ffn_norm_g", 16), ("ple_norm_g", 16), ("c", 8), ("ada_b", 96),
    ("ln_mix_g", 16), ("ln_mix_b", 16), ("ln_ffn_g", 16), ("ln_ffn_b", 16),
    ("ev_conv_w", 12), ("pool_scale", 4), ("lat_g", 5), ("ffn_conv_w", 2 * 3 * 44),
]
PARAM_AT, _n = {}, 0
for _name, _w in PARAM_WIDTHS:
    PARAM_AT[_name] = _n
    _n += _w
N_PARAMS = _n

CONST_WIDTHS = [("ident", P), ("flip", P), ("ones", P), ("ones64", P), ("rot", QK_DIM), ("chunkmask", P),
                ("negdist", S), ("first_counts", 64), ("eps", 2), ("zero", 1)]
CONST_AT, _n = {}, 0
for _name, _w in CONST_WIDTHS:
    CONST_AT[_name] = _n
    _n += _w
N_CONSTS = _n
LATE_WIDTH = HEADS * P + 2 * S


def plan_slots():
    stages, loads, tiles_after = {}, [], []
    tiles = 0

    def stage(name, slots, tiles_of_slot, transfers=1):
        nonlocal tiles
        stages[name] = (len(loads), slots, tiles)
        for j in range(slots):
            loads.append(transfers)
            tiles += tiles_of_slot(j)
            tiles_after.append(tiles + (tiles_of_slot is half and j % 2 == 0))

    two = lambda j: 2
    half = lambda j: j % 2

    def ffn(n):
        stage(f"up{n}", FC, two, 2)
        stage(f"down{n}", 2 * DC, half)

    stage("pw1", DC, two, 2)
    stage("pw2", 4, two)
    ffn(0)
    stage("ple0", DC, two, 2)
    stage("qk", 8, two)
    stage("v", 4, two)
    stage("wo", 4, two)
    ffn(1)
    stage("ple1", DC, two, 2)
    stage("e_index", 2, two)
    stage("e_keyw", 1, two, 3)
    stage("e_qk", 4, two)
    stage("e_v", 2, two)
    stage("e_conv", 4, two, 2)
    stage("e_gate", 2, two)
    stage("e_out", 4, two)
    ffn(2)
    stage("o_in", 5, two)
    stage("o_pool", 1, lambda j: 4)
    stage("o_uq", 4, two)
    stage("o_ukv", 1, lambda j: 12)
    stage("o_out", 4, two)
    ffn(3)
    so_far, landed_due = [0] * RING, []
    for k, n in enumerate(loads):
        so_far[k % RING] += 16 * n
        landed_due.append(so_far[k % RING])
    return stages, landed_due, tiles_after


class Step:

    def __init__(self, first, counter=None, unroll=0):
        self.first, self.counter, self.unroll = first, counter, unroll

    def at(self, f):
        if self.counter is None:
            return f(self.first)
        return f(self.first) + self.counter * (f(self.first + self.unroll) - f(self.first))


def run_steps(engine, n, body, unroll=4, peel=0):
    for j in range(min(peel, n)):
        body(Step(j))
    turns = (n - peel) // unroll
    if turns > 1:
        with engine.Fori(0, turns) as i:
            for s in range(unroll):
                body(Step(peel + s, i, unroll))
    else:
        turns = 0
    for j in range(peel + turns * unroll, n):
        body(Step(j))


class Tally:

    def __init__(self):
        self.seen = {}

    def next(self, sem, n=1):
        self.seen[sem.name] = self.seen.get(sem.name, 0) + n
        return self.seen[sem.name]

    def take(self, sem, n):
        return self.next(sem, n) - n


class Chain:

    def __init__(self, engine, sem):
        self.engine, self.sem = engine, sem
        self.base = self.local = 0
        self.per, self.step_base = 0, 0

    def begin(self, per):
        self.base += self.local
        self.local, self.per = 0, per

    def step(self, st):
        assert self.local in (0, self.per), self.local
        self.local = 0
        self.step_base = st.at(lambda j: j * self.per)

    def end(self, n):
        assert self.local == self.per, self.local
        self.base += n * self.per
        self.local = self.step_base = 0

    def __call__(self, instruction):
        instruction.then_inc(self.sem, 1)
        self.local += 1
        self.engine.wait_ge(self.sem, self.base + self.step_base + self.local)


def build(nc, a, out):
    stages, landed_due, tiles_after = plan_slots()
    with ExitStack() as ctx:
        def sb(name, width):
            return ctx.enter_context(nc.sbuf_tensor(name, [P, width], F32))

        def sem(name):
            return ctx.enter_context(nc.semaphore(name))

        ring = [sb(f"weight_slot{s}", SLOT) for s in range(RING)]
        h = sb("h", DC * S)
        u = sb("u", DC * S)
        act = sb("act", FC * S)
        arena = sb("arena", 11776)
        v_sb = sb("v_sb", DC * S)
        tmp = sb("tmp", 8 * S)
        par = sb("par", N_PARAMS)
        con = sb("con", N_CONSTS)
        p_sb = sb("p_sb", 2 * S)
        mod = sb("mod", 96)
        small = sb("small", 64)
        ps = ctx.enter_context(nc.psum_tensor("ps", [P, 8, S], F32))
        bias_rows = nc.dram_tensor("bias_rows", [HEADS, 640], F32).ap()

        def chunk(t, c, n=1):
            return t[:, c * S:(c + n) * S]

        def pcol(name, i=0):
            at = PARAM_AT[name] + i
            return par[:, at:at + 1]

        def pcol_at(name, st, f):
            if st.counter is None:
                return pcol(name, f(st.first))
            return par[:, bass.ds(st.at(lambda j: PARAM_AT[name] + f(j)), 1)]

        def chunk_at(t, st, f):
            if st.counter is None:
                return chunk(t, f(st.first))
            return t[:, bass.ds(st.at(lambda j: f(j) * S), S)]

        def const(name, width=None):
            at = CONST_AT[name]
            return con[:, at:at + (width or dict(CONST_WIDTHS)[name])]

        ident, flip, ones, ones64 = const("ident"), const("flip"), const("ones"), const("ones64")
        rot, chunkmask, negdist = const("rot"), const("chunkmask"), const("negdist")
        eps_rms, eps_ln = con[:, CONST_AT["eps"]:CONST_AT["eps"] + 1], con[:, CONST_AT["eps"] + 1:CONST_AT["eps"] + 2]
        sq = [chunk(tmp, 0), chunk(tmp, 1)]
        sum1, sum2 = chunk(tmp, 2), chunk(tmp, 3)
        rinv = [chunk(tmp, 4), chunk(tmp, 5)]
        act_tmp = [chunk(tmp, 6), chunk(tmp, 7)]
        ada_slot = [arena[:, s * 2048:(s + 1) * 2048] for s in range(2)]
        ada_acc = arena[:, 4096:4096 + 6 * D]
        tables = arena[:, 0:4096]
        WP = sum((b + 1) * P for b in range(NB))
        p_off = [sum((x + 1) * P for x in range(b)) for b in range(NB)]
        pt_off = [sum((NB - x) * P for x in range(k)) for k in range(NB)]

        def probs(g, comp, b):
            at = 4096 + ((g % 2) * 2 + comp) * WP + p_off[b]
            return arena[:, at:at + (b + 1) * P]

        def probs_t(g, kc):
            at = 4096 + 4 * WP + (g % 2) * WP + pt_off[kc]
            return arena[:, at:at + (NB - kc) * P]

        PADW = CONV - 1 + S
        conv_in = [act[:, i * PADW:(i + 1) * PADW] for i in range(2)]
        E_Q, E_K, E_QI, E_KI, E_CV, E_SC = 0, 4, 8, 12, 13, 17
        e_pad = act[:, 20 * S:20 * S + 2 + S]
        index_w = small[:, 0:32]
        POOLW = 16 + S
        pool_in = [act[:, 16 * S + g * POOLW:16 * S + (g + 1) * POOLW] for g in range(4)]
        lat = [arena[:, 4096 + WP + i * S:4096 + WP + (i + 1) * S] for i in range(2)] + \
              [arena[:, 4096 + 3 * WP + i * S:4096 + 3 * WP + (i + 1) * S] for i in range(2)] + \
              [p_sb[:, 0:S]]
        k_rope_raw = p_sb[:, S:2 * S]
        yc = [chunk(v_sb, 4 + g) for g in range(4)]
        nmax = small[:, 32:40]
        rowsum = small[:, 40:48]
        rowinv = small[:, 48:56]
        lam = small[:, 56:64]
        cond = small[:, 0:8]

        landed = [sem(f"weights_landed{s}") for s in range(RING)]
        ada_landed = [sem(f"ada_landed{s}") for s in range(2)]
        inputs_landed = sem("inputs_landed")
        x_landed = sem("x_landed")
        p_landed = sem("p_landed")
        tables_landed = sem("tables_landed")
        bias_stored = sem("bias_stored")
        out_stored = sem("out_stored")
        tile_done = sem("tile_done")
        tile_used = sem("tile_used")
        h_ready = sem("h_ready")
        squared = sem("squared")
        summed = sem("summed")
        stat_done = sem("stat_done")
        mean_done = sem("mean_done")
        even_ready, odd_ready, index_ready = sem("even_ready"), sem("odd_ready"), sem("index_ready")
        lat_ready = sem("lat_ready")
        rope_used = sem("rope_used")
        rope_raw = sem("rope_raw")
        var_done = sem("var_done")
        rinv_done = sem("rinv_done")
        x_ready = sem("x_ready")
        xa_ready = sem("xa_ready")
        xn_ready = sem("xn_ready")
        act_done = sem("act_done")
        ada_used = sem("ada_used")
        ada_summed = sem("ada_summed")
        mod_done = sem("mod_done")
        mod_ready = sem("mod_ready")
        cond_ready = sem("cond_ready")
        d_chain, a_chain = sem("d_chain"), sem("a_chain")
        qk_normed = sem("qk_normed")
        ln_done = sem("ln_done")
        bias_in = sem("bias_in")
        bias_mm = sem("bias_mm")
        bias_sb = sem("bias_sb")
        lam_in = sem("lam_in")
        lam_mm = sem("lam_mm")
        lam_exp = sem("lam_exp")
        scores_ready = sem("scores_ready")
        max_done = sem("max_done")
        exp_done = sem("exp_done")
        inv_done = sem("inv_done")
        scaled = sem("scaled")
        mixed = sem("mixed")
        turned = sem("turned")
        turned_dve, turned_act = sem("turned_dve"), sem("turned_act")
        o_done = sem("o_done")
        o_copied = sem("o_copied")
        relu_done = sem("relu_done")
        relu_used = sem("relu_used")
        rope_mm = sem("rope_mm")
        pool_ready = sem("pool_ready")

        def q_chunk(c):
            return chunk(act, c)

        def head_rows(h_, width):
            return slice(64 * (h_ % 2), 64 * (h_ % 2) + 64)

        def tok(b):
            return slice(b * P, (b + 1) * P)

        ATT = {
            "diff": dict(heads=HEADS, comps=2, norm=True),
            "dsa": dict(heads=HEADS, comps=1, norm=False),
            "mla": dict(heads=HEADS, comps=1, norm=False),
        }

        block = ctx.enter_context(nc.Block())

        @block.sync
        def _(sp):
            n = Tally()
            sp.dma_start(par[:], a["params"]).then_inc(inputs_landed, 16)
            sp.dma_start(con[:], a["consts"]).then_inc(inputs_landed, 16)
            for c in range(DC):
                sp.dma_start(chunk(h, c), a["x_t"][c * P:(c + 1) * P]).then_inc(x_landed, 16)
            sp.dma_start(v_sb[0:BUCKETS, 0:HEADS], a["rel_bias"]).then_inc(inputs_landed, 16)
            sp.dma_start(v_sb[0:BUCKETS + 1, 8:648], a["bucket_of"]).then_inc(inputs_landed, 16)

            def load(name, sources, unroll=4, extra=None):
                k0, slots, _ = stages[name]

                def body(st):
                    s = (k0 + st.first) % RING
                    if k0 + st.first >= RING:
                        sp.wait_ge(tile_done, st.at(lambda j: tiles_after[k0 + j - RING]))
                    for dst, src in sources(st, ring[s]):
                        sp.dma_start(dst, src).then_inc(landed[s], 16)
                    if extra:
                        extra(st)

                run_steps(sp, slots, body, unroll, peel=4)

            def columns(w, st, f, width=256):
                w = w.rearrange("(c p) n -> p c n", p=P)
                if st.counter is None:
                    return w[:, :, f(st.first):f(st.first) + width]
                return w[:, :, bass.ds(st.at(f), width)]

            def k_by(slot, kc, width):
                return slot[:, 0:kc * width].rearrange("p (c n) -> p c n", c=kc)

            def plain(w, at=0, kc=DC, width=256):
                return lambda st, slot: [(k_by(slot, kc, width), columns(w, st, lambda j: at + j * width, width))]

            def pair(wa, wb, at_a=0, at_b=0, kb=DC):
                def f(st, slot):
                    return [
                        (k_by(slot[:, 0:DC * P], DC, P), columns(wa, st, lambda j: at_a + j * P, P)),
                        (k_by(slot[:, DC * P:], kb, P), columns(wb, st, lambda j: at_b + j * P, P)),
                    ]
                return f

            def down(w):
                w = w.rearrange("(z c p) n -> z p c n", p=P, z=2)

                def f(st, slot):
                    z = st.first % 2
                    src = w[z]
                    if st.counter is None:
                        t = st.first // 2
                        src = src[:, :, t * P:(t + 1) * P]
                    else:
                        src = src[:, :, bass.ds(st.at(lambda j: (j - z) // 2 * P), P)]
                    return [(k_by(slot, FC // 2, P), src)]
                return f

            def ada(layer):
                w = a["ada_w"][layer].rearrange("(c p) n -> p c n", p=P)
                used0 = n.take(ada_used, 24)

                def one(st, lag=0):
                    s, slot = (st.first + lag) % 4, (st.first + lag) % 2
                    idx = layer * 24
                    sp.wait_ge(ada_used, st.at(lambda j: used0 + j + lag + 1))
                    if st.counter is None:
                        i = (st.first + lag) // 4
                        src = w[:, 2 * s:2 * s + 2, i * D:(i + 1) * D]
                    else:
                        src = w[:, 2 * s:2 * s + 2, bass.ds(st.at(lambda j: (j - s) // 4 * D), D)]
                    sp.dma_start(ada_slot[slot].rearrange("p (c n) -> p c n", c=2), src).then_inc(ada_landed[slot], 16)

                def f(st):
                    one(st)
                    if st.counter is None and st.first == FC - 1:
                        one(st, 1)
                        one(st, 2)
                return f

            def ffn(i, gate, up, dn, at_b=0, extra=None):
                load(f"up{i}", pair(gate, up, 0, at_b), extra=extra)
                load(f"down{i}", down(dn), unroll=8)

            load("pw1", pair(a["conv_w_pw1"], a["conv_w_pw1"], 0, D))
            sp.wait_ge(bias_sb, 1)
            sp.dma_start(bias_rows, act[0:HEADS, 20 * S:20 * S + 640]).then_inc(bias_stored, 16)
            load("pw2", plain(a["conv_w_pw2"]))
            ffn(0, a["ffn_w_gate"][0], a["ffn_w_up"][0], a["ffn_w_down"][0], extra=ada(0))
            sp.dma_start(p_sb[:].rearrange("p (c n) -> p c n", c=2), a["p_t"][0].rearrange("(c p) n -> p c n", p=P)).then_inc(p_landed, 16)
            load("ple0", pair(a["ple_w_gate"][0], a["ple_w_proj"][0], kb=2))
            sp.wait_ge(bias_stored, 16)
            sp.wait_ge(mod_ready, n.next(mod_ready))
            for hd in range(HEADS):
                sp.dma_start(tables[:, hd * S:(hd + 1) * S],
                             bass.AP(bias_rows.tensor, hd * 640, [[1, P], [1, S]])).then_inc(tables_landed, 16)
            load("qk", plain(a["attn_w_qkv"]))
            load("v", plain(a["attn_w_qkv"], 2 * D))
            load("wo", plain(a["attn_w_o"]))
            sp.dma_start(p_sb[:].rearrange("p (c n) -> p c n", c=2), a["p_t"][1].rearrange("(c p) n -> p c n", p=P)).then_inc(p_landed, 16)
            sp.wait_ge(tile_done, stages["wo"][2] + 1)
            ffn(1, a["ffn_w_gate"][1], a["ffn_w_up"][1], a["ffn_w_down"][1], extra=ada(1))
            load("ple1", pair(a["ple_w_gate"][1], a["ple_w_proj"][1], kb=2))
            sp.wait_ge(mod_ready, n.next(mod_ready))
            sp.dma_start(tables[:, 2048:4096], a["late"]).then_inc(tables_landed, 16)
            w = a["ev_w_in"]
            load("e_index", plain(w, 1536))

            def key_and_w(st, slot):
                to = slot[:, 0:DC * 136].rearrange("p (c n) -> p c n", c=DC)
                wr = w.rearrange("(c p) n -> p c n", p=P)
                return [(to[:, :, 0:64], wr[:, :, 2048:2112]), (to[:, :, 64:128], wr[:, :, 2048:2112]),
                        (to[:, :, 128:136], wr[:, :, 2112:2120])]

            load("e_keyw", key_and_w)
            load("e_qk", plain(w, 0))
            load("e_v", plain(w, 1024))
            load("e_conv", pair(w, w, 2632, 3144))
            load("e_gate", plain(w, 2120))
            load("e_out", plain(a["ev_w_out"]))
            ffn(2, a["ffn_w_up2"][0], a["ffn_w_up2"][0], a["ffn_w_down2"][0], at_b=FF)
            w2 = a["od_w_in"].rearrange("(c p) n -> p c n", p=P)

            def odd_in(st, slot):
                width = 256 if st.first < 4 else 160
                return [(k_by(slot, DC, width), w2[:, :, st.first * 256:st.first * 256 + width])]

            load("o_in", odd_in, unroll=8)
            load("o_pool", lambda st, slot: [(k_by(slot, 4, P), a["pool_w"].rearrange("g c d -> c g d"))])
            load("o_uq", plain(a["w_uq"], 0, 3, 192))
            load("o_ukv", lambda st, slot: [(k_by(slot, 2, D), a["w_ukv"].rearrange("(c p) n -> p c n", p=P))])
            load("o_out", plain(a["od_w_out"]))
            ffn(3, a["ffn_w_up2"][1], a["ffn_w_up2"][1], a["ffn_w_down2"][1], at_b=FF)
            for c in range(DC):
                sp.wait_ge(xa_ready, 5 * DC + c + 1)
                sp.dma_start(out[c * P:(c + 1) * P], chunk(h, c)).then_inc(out_stored, 16)
            sp.wait_ge(out_stored, 16 * DC)

        @block.tensor
        def _(pe):
            n = Tally()
            pe.sem_inc(tile_used, BANKS)
            pe.wait_ge(inputs_landed, 64)

            def slot_of(name, st):
                k0 = stages[name][0]
                s = (k0 + st.first) % RING
                pe.wait_ge(landed[s], st.at(lambda j: landed_due[k0 + j]))
                return ring[s]

            def open_tile(t0, st, per, i):
                t = lambda j: t0 + per * j + i
                pe.wait_ge(tile_used, st.at(lambda j: t(j) + 1))
                return ps[:, t(st.first) % BANKS]

            def stage_gemm(name, x, kc=(DC, DC), chunk_sem=x_ready, unroll=4, wait_all=False, first_wait=None):
                t0 = stages[name][2]
                if wait_all and chunk_sem is not None:
                    pe.wait_ge(chunk_sem, n.next(chunk_sem, DC))

                def body(st):
                    w = slot_of(name, st)
                    for i in range(2):
                        bank = open_tile(t0, st, 2, i)
                        for k in range(kc[i]):
                            if st.first == 0 and i == 0 and chunk_sem is not None and not wait_all:
                                pe.wait_ge(chunk_sem, n.next(chunk_sem))
                            if st.first == 0 and i == 1 and k == 0 and first_wait:
                                pe.wait_ge(*first_wait)
                            lhs = w_cols(w, i, k)
                            mm = pe.matmul(bank, lhs, x[i](k), start=k == 0, stop=k == kc[i] - 1)
                        mm.then_inc(tile_done, 1)

                w_cols = plain_cols if name in PLAIN else pair_cols
                run_steps(pe, stages[name][1], body, unroll, peel=1)

            PLAIN = ("pw2", "qk", "wo", "e_index", "e_qk", "e_gate", "e_out", "o_out")

            def plain_cols(w, i, k):
                return w[:, k * 256 + i * P:k * 256 + (i + 1) * P]

            def pair_cols(w, i, k):
                return w[:, i * DC * P + k * P:i * DC * P + (k + 1) * P]

            xu = lambda k: chunk(u, k)

            def stage_down(name):
                k0, _, t0 = stages[name]

                def body(st):
                    bank = open_tile(t0, st, 1, 0)
                    for z in range(2):
                        s = (k0 + 2 * st.first + z) % RING
                        pe.wait_ge(landed[s], st.at(lambda j: landed_due[k0 + 2 * j + z]))
                        for k in range(FC // 2):
                            kk = z * (FC // 2) + k
                            if st.first == 0:
                                pe.wait_ge(x_ready, n.next(x_ready))
                            mm = pe.matmul(bank, ring[s][:, k * P:(k + 1) * P], chunk(act, kk),
                                           start=kk == 0, stop=kk == FC - 1)
                    mm.then_inc(tile_done, 1)

                run_steps(pe, DC, body, 4, peel=1)

            def rms_stat(adds=9):
                n.take(squared, DC)
                pe.wait_ge(summed, n.next(summed, adds))
                pe.matmul(ps[:, 4], ones, sum2, start=True, stop=True).then_inc(stat_done, 1)

            def ln_stat():
                n.take(squared, DC)
                pe.wait_ge(summed, n.next(summed, 18))
                pe.matmul(ps[:, 4], ones, sum1, start=True, stop=True).then_inc(stat_done, 1)
                pe.matmul(ps[:, 5], ones, sum2, start=True, stop=True).then_inc(stat_done, 1)

            def mod_vector(layer):
                pe.wait_ge(ada_summed, n.next(ada_summed))
                for c in range(48):
                    mm = pe.matmul(ps[:, 6, c:c + 1], ada_acc[:, c * P:(c + 1) * P], ones[:, 0:1], start=True, stop=True)
                mm.then_inc(mod_done, 1)

            def values(name, cols=256):
                t0 = stages[name][2]

                def body(st):
                    w = slot_of(name, st)
                    for i in range(2):
                        bank = open_tile(t0, st, 2, i)
                        for b in range(2):
                            for k in range(DC):
                                mm = pe.matmul(bank[:, b * 256:(b + 1) * 256],
                                               chunk(u, k)[:, tok(2 * i + b)], w[:, k * 256:(k + 1) * 256],
                                               start=k == 0, stop=k == DC - 1)
                        mm.then_inc(tile_done, 1)

                run_steps(pe, stages[name][1], body, 4, peel=1)

            def attention(kind):
                spec = ATT[kind]
                G, C = spec["heads"], spec["comps"]
                item = 0
                pe.wait_ge(tile_used, {"diff": stages["wo"][2], "dsa": stages["e_out"][2], "mla": stages["o_out"][2]}[kind] + BANKS)

                def score_tiles(g):
                    nonlocal item
                    for comp in range(C):
                        for b in range(NB):
                            nk = (b + 1) * P
                            if item >= 4:
                                pe.wait_ge(exp_done, n.next(exp_done))
                            bank = ps[:, 4 + item % 4, 0:nk]
                            at = 384 - b * P
                            if kind == "diff":
                                r = slice(64 * comp, 64 * comp + 64)
                                pe.matmul(bank, q_chunk(g)[r, tok(b)], q_chunk(8 + g)[r, 0:nk], start=True, stop=False)
                                mm = pe.matmul(bank, flip, tables[:, g * S + at:g * S + at + nk], start=False, stop=True)
                            elif kind == "dsa":
                                r = slice(64 * (g % 2), 64 * (g % 2) + 64)
                                pe.matmul(bank, q_chunk(E_Q + g // 2)[r, tok(b)], q_chunk(E_K + g // 2)[r, 0:nk], start=True, stop=False)
                                pe.matmul(bank, tables[:, 2048 + g * P:2048 + (g + 1) * P], negdist[:, at:at + nk], start=False, stop=False)
                                mm = pe.matmul(bank, ident, tables[:, b * S:b * S + nk], start=False, stop=True)
                            else:
                                pe.matmul(bank, act[0:QK_DIM, g * S + b * P:g * S + (b + 1) * P],
                                          act[0:QK_DIM, (8 + g) * S:(8 + g) * S + nk], start=True, stop=False)
                                mm = pe.matmul(ps[:, 4 + item % 4, nk - P:nk], ident, chunkmask, start=False, stop=True)
                            mm.then_inc(scores_ready, 1)
                            item += 1

                def turn(g):
                    if kind == "diff":
                        n.take(scaled, 4)
                        pe.wait_ge(mixed, n.next(mixed, 4))
                    else:
                        pe.wait_ge(scaled, n.next(scaled, 4))
                    for kc in range(NB):
                        if g > 0 or kc >= 2:
                            copied = (turned_act, turned_dve, turned_dve, turned_act)[kc]
                            pe.wait_ge(copied, turned_at + 2 * g + kc // 2)
                        for b in range(kc, NB):
                            mm = pe.transpose(ps[:, kc % 2, (b - kc) * P:(b - kc + 1) * P],
                                              probs(g, 0, b)[:, kc * P:(kc + 1) * P], ident)
                        mm.then_inc(turned, 1)

                def weigh(g):
                    pe.wait_ge(turned_dve, 2 * (g + 1) + turned_at)
                    pe.wait_ge(turned_act, 2 * (g + 1) + turned_at)
                    dim = P if kind == "diff" else 64
                    r0 = 0 if kind == "diff" else 64 * (g % 2)
                    if kind == "diff" or g % 2 == 0:
                        if g > 0:
                            pe.wait_ge(o_copied, n.next(o_copied))
                    for kc in range(NB):
                        if kind == "diff":
                            val = v_sb[:, kc * D + g * P:kc * D + (g + 1) * P]
                        else:
                            val = v_sb[:, kc * S + g * 64:kc * S + (g + 1) * 64]
                        mm = pe.matmul(ps[r0:r0 + dim, 2, kc * P:S], val, probs_t(g, kc), start=kc == 0, stop=kc == NB - 1)
                    mm.then_inc(o_done, 1)

                def stat(g):
                    pe.wait_ge(squared, n.next(squared))
                    if g > 0:
                        pe.wait_ge(ln_done, n.next(ln_done))
                    pe.matmul(ps[:, 3], ones, sq[g % 2], start=True, stop=True).then_inc(stat_done, 1)

                turned_at = 2 * HEADS * {"diff": 0, "dsa": 1, "mla": 2}[kind]
                for g in range(G + 3):
                    if g < G:
                        score_tiles(g)
                    if 0 <= g - 1 < G:
                        turn(g - 1)
                    if 0 <= g - 2 < G:
                        weigh(g - 2)
                    if spec["norm"] and 0 <= g - 3 < G:
                        stat(g - 3)
                n.next(exp_done, 4)
                n.next(o_copied)
                if spec["norm"]:
                    n.next(ln_done)

            pe.wait_ge(bias_in, n.next(bias_in))
            pe.matmul(ps[0:HEADS, 6], v_sb[0:BUCKETS + 1, 0:HEADS], v_sb[0:BUCKETS + 1, 8:520], start=True, stop=True)
            pe.matmul(ps[0:HEADS, 7, 0:P], v_sb[0:BUCKETS + 1, 0:HEADS], v_sb[0:BUCKETS + 1, 520:648], start=True, stop=True).then_inc(bias_mm, 1)
            pe.wait_ge(lam_in, 1)
            pe.matmul(ps[:, 5, 0:2], ones[0:64, :], lam[0:64, 0:2], start=True, stop=True).then_inc(lam_mm, 1)
            rms_stat()
            stage_gemm("pw1", (xu, xu))
            ln_stat()
            stage_gemm("pw2", (xu, xu), chunk_sem=xa_ready)
            for i in range(2):
                rms_stat()
                stage_gemm(f"up{i}", (xu, xu))
                stage_down(f"down{i}")
                mod_vector(i)
                rms_stat()
                pe.wait_ge(p_landed, 16 * (i + 1))
                stage_gemm(f"ple{i}", (xu, lambda k: p_sb[:, k * S:(k + 1) * S]), kc=(DC, 2))
                if i:
                    break
                rms_stat()
                t0 = stages["qk"][2]
                for j in range(9):
                    if j < 8:
                        w = slot_of("qk", Step(j))
                        for i2 in range(2):
                            bank = open_tile(t0, Step(j), 2, i2)
                            for k in range(DC):
                                if j == 0 and i2 == 0:
                                    pe.wait_ge(x_ready, n.next(x_ready))
                                mm = pe.matmul(bank, plain_cols(w, i2, k), chunk(u, k), start=k == 0, stop=k == DC - 1)
                            mm.then_inc(tile_done, 1)
                    if j >= 1:
                        for t in (2 * j - 2, 2 * j - 1):
                            pe.wait_ge(squared, n.next(squared))
                            if t >= 2:
                                pe.wait_ge(ln_done, n.next(ln_done))
                            pe.matmul(ps[:, 4 + t % 2], ones64, sq[t % 2], start=True, stop=True).then_inc(stat_done, 1)
                n.next(ln_done, 2)
                values("v")
                pe.wait_ge(qk_normed, 16)
                pe.wait_ge(tables_landed, 16 * HEADS)
                attention("diff")
                stage_gemm("wo", (xu, xu), wait_all=True)
            stage_gemm("e_index", (xu, xu), chunk_sem=xa_ready)
            t0 = stages["e_keyw"][2]
            w = slot_of("e_keyw", Step(0))
            bank = open_tile(t0, Step(0), 2, 0)
            for k in range(DC):
                mm = pe.matmul(bank, w[:, k * 136:k * 136 + P], chunk(u, k), start=k == 0, stop=k == DC - 1)
            mm.then_inc(tile_done, 1)
            bank = open_tile(t0, Step(0), 2, 1)
            for b in range(NB):
                for k in range(DC):
                    mm = pe.matmul(bank[:, b * 8:(b + 1) * 8], chunk(u, k)[:, tok(b)], w[:, k * 136 + P:(k + 1) * 136],
                                   start=k == 0, stop=k == DC - 1)
            mm.then_inc(tile_done, 1)
            pe.wait_ge(index_ready, 1)
            item = 0
            for b in range(1, NB):
                for hd in range(HEADS):
                    if item >= 4:
                        pe.wait_ge(relu_done, n.next(relu_done))
                    r = slice(64 * (hd % 2), 64 * (hd % 2) + 64)
                    pe.matmul(ps[:, 4 + item % 4, 0:(b + 1) * P], q_chunk(E_QI + hd // 2)[r, tok(b)],
                              q_chunk(E_KI)[r, 0:(b + 1) * P], start=True, stop=True).then_inc(scores_ready, 1)
                    item += 1
            n.next(relu_done, 4)
            stage_gemm("e_qk", (xu, xu), chunk_sem=None)
            values("e_v")
            stage_gemm("e_conv", (xu, xu), chunk_sem=None)
            stage_gemm("e_gate", (xu, xu), chunk_sem=None)
            pe.wait_ge(relu_done, n.seen["relu_done"])
            pe.wait_ge(tables_landed, 16 * HEADS + 16)
            pe.wait_ge(even_ready, 1)
            attention("dsa")
            e_x = lambda k: chunk(u, k) if k < 4 else chunk(act, E_CV + k - 4)
            pe.wait_ge(o_copied, n.seen["o_copied"])
            stage_gemm("e_out", (e_x, e_x), chunk_sem=None)
            ln_stat()
            stage_gemm("up2", (xu, xu), chunk_sem=xa_ready)
            stage_down("down2")
            ln_stat()
            def odd_in():
                t0 = stages["o_in"][2]
                for j in range(5):
                    w = slot_of("o_in", Step(j))
                    width = 256 if j < 4 else 160
                    for i in range(2):
                        bank = open_tile(t0, Step(j), 2, i)
                        for k in range(DC):
                            if j == 0 and i == 0:
                                pe.wait_ge(xa_ready, n.next(xa_ready))
                            if j == 4 and i == 1:
                                mm = pe.matmul(bank[0:96], w[:, k * width + 64:k * width + 160], chunk(u, k), start=k == 0, stop=k == DC - 1)
                            else:
                                mm = pe.matmul(bank, w[:, k * width + i * P:k * width + (i + 1) * P], chunk(u, k), start=k == 0, stop=k == DC - 1)
                        mm.then_inc(tile_done, 1)
            odd_in()
            for i in range(5):
                pe.wait_ge(squared, n.next(squared))
                mm = pe.matmul(ps[:, 4 if i < 3 else 5], ones, sq[i % 2], start=i in (0, 3), stop=i in (2, 4))
                mm.then_inc(stat_done, 1)
            pe.wait_ge(pool_ready, 4)
            w = slot_of("o_pool", Step(0))
            t0 = stages["o_pool"][2]
            for g in range(4):
                bank = open_tile(t0, Step(0), 4, g)
                pe.matmul(bank, w[:, g * P:(g + 1) * P], pool_in[g][:, 16:], start=True, stop=True).then_inc(tile_done, 1)
            pe.wait_ge(rope_raw, 1)
            pe.matmul(ps[0:QK_DIM, 6], rot[0:QK_DIM], k_rope_raw[0:QK_DIM], start=True, stop=True).then_inc(rope_mm, 1)
            t0 = stages["o_uq"][2]
            pe.wait_ge(lat_ready, 5)
            for j in range(5):
                if j < 4:
                    w = slot_of("o_uq", Step(j))
                    for i in range(2):
                        bank = open_tile(t0, Step(j), 2, i)
                        for k in range(3):
                            mm = pe.matmul(bank[0:QK_DIM], w[:, k * 192 + i * QK_DIM:k * 192 + (i + 1) * QK_DIM], lat[k], start=k == 0, stop=k == 2)
                        mm.then_inc(tile_done, 1)
                if j >= 1:
                    for hd in (2 * j - 2, 2 * j - 1):
                        pe.wait_ge(rope_raw, hd + 2)
                        if hd >= 1:
                            pe.wait_ge(rope_used, hd)
                        pe.matmul(ps[0:QK_DIM, 6 + (hd + 1) % 2], rot[0:QK_DIM], act[0:QK_DIM, hd * S:(hd + 1) * S], start=True, stop=True).then_inc(rope_mm, 1)
            w = slot_of("o_ukv", Step(0))
            t0 = stages["o_ukv"][2]
            wk = w[:].rearrange("p (c h n) -> p c h n", c=2, h=HEADS)
            for hd in range(HEADS):
                bank = open_tile(t0, Step(0), 12, hd)
                for k in range(2):
                    mm = pe.matmul(bank[0:NOPE], wk[:, k, hd, 0:NOPE], lat[3 + k], start=k == 0, stop=k == 1)
                mm.then_inc(tile_done, 1)
            for b in range(NB):
                bank = open_tile(t0, Step(0), 12, HEADS + b)
                for k in range(2):
                    mm = pe.matmul(bank.rearrange("p (h n) -> p h n", h=HEADS), lat[3 + k][:, tok(b)], wk[:, k, :, NOPE:P], start=k == 0, stop=k == 1)
                mm.then_inc(tile_done, 1)
            pe.wait_ge(odd_ready, 1)
            attention("mla")
            o_x = lambda k: yc[k] if k < 4 else chunk(u, k - 4)
            pe.wait_ge(o_copied, n.seen["o_copied"])
            stage_gemm("o_out", (o_x, o_x), chunk_sem=None)
            ln_stat()
            stage_gemm("up3", (xu, xu), chunk_sem=xa_ready)
            stage_down("down3")
            ln_stat()

        @block.vector
        def _(dve):
            n = Tally()
            link = Chain(dve, d_chain)
            items = [0]

            def read_tile(st, f):
                dve.wait_ge(tile_done, st.at(lambda j: f(j) + 1))
                return ps[:, f(st.first) % BANKS]

            def one_tile(t):
                return read_tile(Step(0), lambda _: t)

            def sums_begin(ln):
                dve.memset(sum2, 0.0).then_inc(summed, 1)
                if ln:
                    dve.memset(sum1, 0.0).then_inc(summed, 1)
                return n.take(summed, 18 if ln else 9), n.take(squared, DC)

            def sums_add(st, base, src, ln):
                s0, q0 = base
                if ln:
                    dve.wait_ge(summed, st.at(lambda j: s0 + 2 + 2 * j))
                    dve.tensor_tensor(sum1, sum1, src, ALU.add).then_inc(summed, 1)
                dve.wait_ge(squared, st.at(lambda j: q0 + j + 1))
                if not ln:
                    dve.wait_ge(summed, st.at(lambda j: s0 + 1 + j))
                dve.tensor_tensor(sum2, sum2, sq[st.first % 2], ALU.add).then_inc(summed, 1)

            def rms_apply(gain, gain_at):
                n.take(x_ready, DC)
                dve.wait_ge(rinv_done, n.next(rinv_done))
                for c in range(DC):
                    dve.scalar_tensor_tensor(chunk(u, c), chunk(h, c), pcol(gain, gain_at + c), rinv[0],
                                             ALU.mult, ALU.mult).then_inc(x_ready, 1)

            def ln_apply(src, gain, gain_at):
                mean, var = sum1, sum2
                x0 = n.take(xa_ready, DC)
                dve.wait_ge(mean_done, n.next(mean_done))
                link(dve.tensor_tensor(rinv[1], mean, mean, ALU.mult))
                link(dve.scalar_tensor_tensor(var, ps[:, 5], 1.0 / D, rinv[1], ALU.mult, ALU.subtract))
                link(dve.tensor_scalar(var, var, 0.0, None, ALU.max))
                dve.sem_inc(var_done, 1)
                dve.wait_ge(rinv_done, n.next(rinv_done))
                for c in range(DC):
                    t = act_tmp[c % 2]
                    if x0 + c >= 2:
                        dve.wait_ge(xa_ready, x0 + c - 1)
                    link(dve.tensor_tensor(t, chunk(src, c), mean, ALU.subtract))
                    dve.scalar_tensor_tensor(t, t, pcol(gain, gain_at + c), rinv[0],
                                             ALU.mult, ALU.mult).then_inc(xn_ready, 1)

            def residual(name, bias=None, gate=None):
                t0 = stages[name][2]
                ln = gate is not None
                base = sums_begin(ln)
                link.begin(1 if ln else 0)

                def body(st):
                    link.step(st)
                    bank = read_tile(st, lambda j: t0 + j)
                    hc = chunk_at(h, st, lambda j: j)
                    if ln:
                        t = act_tmp[st.first % 2]
                        g = mod[:, gate + st.first:gate + st.first + 1] if st.counter is None else \
                            mod[:, bass.ds(st.at(lambda j: gate + j), 1)]
                        link(dve.tensor_scalar(t, bank, g, None, ALU.mult))
                        dve.scalar_tensor_tensor(hc, hc, DN_ALPHA, t, ALU.mult, ALU.add).then_inc(tile_used, 1)
                        dve.wait_ge(tile_used, st.at(lambda j: BANKS + t0 + j + 1))
                    elif bias is not None:
                        dve.scalar_tensor_tensor(hc, bank, pcol_at(bias, st, lambda j: j), hc,
                                                 ALU.add, ALU.add).then_inc(tile_used, 1)
                    else:
                        dve.tensor_tensor(hc, bank, hc, ALU.add).then_inc(tile_used, 1)
                    sums_add(st, base, hc, ln)

                run_steps(dve, DC, body, 4)
                link.end(DC)

            def up_stage(i):
                t0 = stages[f"up{i}"][2]
                a0, x0 = n.take(act_done, FC), n.take(x_ready, FC)
                dve.wait_ge(cond_ready, 1)

                def ada_step(st, lag=0):
                    s, slot = (st.first + lag) % 4, (st.first + lag) % 2
                    dve.wait_ge(ada_landed[slot], st.at(lambda j: 16 * ((i * 24 + j + lag) // 2 + 1)))
                    rows = ada_slot[slot]
                    if st.counter is None:
                        at = (st.first + lag) // 4 * D
                        acc = ada_acc[:, at:at + D]
                    else:
                        acc = arena[:, bass.ds(st.at(lambda j: 4096 + (j - s) // 4 * D), D)]
                    if s == 0:
                        link(dve.tensor_scalar(acc, rows[:, 0:D], cond[:, 0:1], None, ALU.mult))
                    else:
                        link(dve.scalar_tensor_tensor(acc, rows[:, 0:D], cond[:, 2 * s:2 * s + 1], acc, ALU.mult, ALU.add))
                    link(dve.scalar_tensor_tensor(acc, rows[:, D:2 * D], cond[:, 2 * s + 1:2 * s + 2], acc, ALU.mult, ALU.add))
                    dve.sem_inc(ada_used, 1)

                def body(st):
                    link.step(st)
                    bank = read_tile(st, lambda j: t0 + 2 * j + 1)
                    dve.wait_ge(act_done, st.at(lambda j: a0 + j + 1))
                    dve.tensor_tensor(chunk_at(act, st, lambda j: j), act_tmp[st.first % 2], bank,
                                      ALU.mult).then_inc(x_ready, 1)
                    dve.wait_ge(x_ready, st.at(lambda j: x0 + j + 1))
                    dve.sem_inc(tile_used, 2)
                    ada_step(st)

                link.begin(2)
                run_steps(dve, FC, body, 4)
                link.end(FC)
                link.begin(0)
                for lag in (1, 2):
                    ada_step(Step(FC - 1), lag)
                dve.sem_inc(ada_summed, 1)

            def up_conv_stage(i, layer):
                t0 = stages[f"up{i}"][2]
                a0, x0 = n.take(act_done, 3 * FC), n.take(x_ready, FC)

                def body(st):
                    link.step(st)
                    par_ = st.first % 2
                    tiles = [(act_tmp[par_], 0), (rinv[par_], FC)]
                    banks = [read_tile(st, lambda j: t0 + 2 * j), read_tile(st, lambda j: t0 + 2 * j + 1)]
                    dve.wait_ge(act_done, st.at(lambda j: a0 + 3 * j + 2))
                    for back in (1, 2):
                        for (y, at), bank in zip(tiles, banks):
                            tap = pcol_at("ffn_conv_w", st, lambda j: layer * 132 + (at + j) * 3 + 2 - back)
                            link(dve.scalar_tensor_tensor(y[:, back:], bank[:, 0:S - back], tap, y[:, back:], ALU.mult, ALU.add))
                    dve.sem_inc(h_ready, 1)
                    dve.sem_inc(tile_used, 2)
                    dve.wait_ge(act_done, st.at(lambda j: a0 + 3 * j + 3))
                    dve.tensor_tensor(chunk_at(act, st, lambda j: j), act_tmp[par_], rinv[par_], ALU.mult).then_inc(x_ready, 1)

                link.begin(4)
                run_steps(dve, FC, body, 4)
                link.end(FC)

            def ple_stage(i, sums):
                t0 = stages[f"ple{i}"][2]
                a0 = n.take(act_done, DC)
                if sums:
                    base = sums_begin(False)
                link.begin(1)

                def body(st):
                    link.step(st)
                    bank = read_tile(st, lambda j: t0 + 2 * j + 1)
                    dve.wait_ge(act_done, st.at(lambda j: a0 + j + 1))
                    t = act_tmp[st.first % 2]
                    link(dve.tensor_tensor(t, t, bank, ALU.mult))
                    hc = chunk_at(h, st, lambda j: j)
                    dve.tensor_tensor(hc, hc, t, ALU.add).then_inc(tile_used, 2)
                    if sums:
                        sums_add(st, base, hc, False)

                run_steps(dve, DC, body, 4)
                link.end(DC)

            def mod_stage(layer):
                link.begin(0)
                dve.wait_ge(mod_done, n.next(mod_done))
                m = mod[:, layer * 48:(layer + 1) * 48]
                at = PARAM_AT["ada_b"] + layer * 48
                link(dve.tensor_tensor(m, ps[:, 6, 0:48], par[:, at:at + 48], ALU.add))
                link(dve.tensor_scalar(m[:, 8:24], m[:, 8:24], 1.0, None, ALU.add))
                link(dve.tensor_scalar(m[:, 32:48], m[:, 32:48], 1.0, None, ALU.add))
                dve.sem_inc(mod_ready, 1)

            def attention(kind):
                link.begin(0)
                G, C, norm = ATT[kind]["heads"], ATT[kind]["comps"], ATT[kind]["norm"]
                e0, t0 = n.take(exp_done, 4 * C * G), n.take(turned, 4 * G)
                o0, s0 = n.take(o_done, G), n.take(scaled, 4 * G)
                n.take(squared, G if norm else 0)
                for g in range(G + 3):
                    if g < G:
                        for i in range(4 * C):
                            b = i % 4
                            dve.wait_ge(scores_ready, n.next(scores_ready))
                            if g > 0:
                                dve.wait_ge(exp_done, e0 + (g - 1) * 4 * C + i + 1)
                            dve.tensor_reduce(nmax[:, i:i + 1], ps[:, 4 + items[0] % 4, 0:(b + 1) * P],
                                              AX.X, ALU.max, negate=True).then_inc(max_done, 1)
                            items[0] += 1
                    if 0 <= g - 1 < G:
                        for kc in (0, 3):
                            dve.wait_ge(turned, t0 + 4 * (g - 1) + kc + 1)
                            if g - 1 >= 2:
                                dve.wait_ge(o_done, o0 + g - 2)
                            dve.tensor_copy(probs_t(g - 1, kc), ps[:, kc % 2, 0:(NB - kc) * P]).then_inc(turned_dve, 1)
                    if 0 <= g - 2 < G:
                        dve.wait_ge(o_done, o0 + g - 1)
                        if kind == "diff":
                            dve.tensor_copy(chunk(u, g - 2), ps[:, 2]).then_inc(o_copied, 1)
                        elif g % 2 == 1:
                            dve.tensor_copy(chunk(u, (g - 2) // 2), ps[:, 2]).then_inc(o_copied, 1)
                    if norm and 0 <= g - 3 < G:
                        dve.wait_ge(rinv_done, n.next(rinv_done))
                        n.take(x_ready, 1)
                        dve.scalar_tensor_tensor(chunk(u, g - 3), chunk(u, g - 3), lam[:, 7:8], rinv[(g - 3) % 2],
                                                 ALU.mult, ALU.mult).then_inc(x_ready, 1)
                    if g < G:
                        dve.wait_ge(exp_done, e0 + (g + 1) * 4 * C)
                        if g > 0:
                            dve.wait_ge(scaled, s0 + 4 * g)
                        if C == 2:
                            link(dve.reciprocal(rowinv[:, 4:8], rowsum[:, 4:8]))
                            link(dve.tensor_scalar(rowinv[:, 4:8], rowinv[:, 4:8], lam[:, 6:7], None, ALU.mult))
                        dve.reciprocal(rowinv[:, 0:4], rowsum[:, 0:4]).then_inc(inv_done, 1)
                        if C == 2:
                            for b in range(NB):
                                dve.wait_ge(scaled, s0 + 4 * g + b + 1)
                                dve.scalar_tensor_tensor(probs(g, 0, b), probs(g, 1, b), rowinv[:, 4 + b:5 + b],
                                                         probs(g, 0, b), ALU.mult, ALU.add).then_inc(mixed, 1)

            dve.wait_ge(inputs_landed, 64)
            dve.memset(v_sb[BUCKETS:BUCKETS + 1, 0:HEADS], NEG).then_inc(bias_in, 1)
            lq = PARAM_AT["lambda"]
            link(dve.tensor_scalar(pcol("q_norm_g"), pcol("q_norm_g"), 64 ** -0.5, None, ALU.mult))
            link(dve.tensor_tensor(lam[:, 0:1], par[:, lq:lq + 1], par[:, lq + 1:lq + 2], ALU.mult))
            dve.tensor_tensor(lam[:, 1:2], par[:, lq + 2:lq + 3], par[:, lq + 3:lq + 4], ALU.mult).then_inc(lam_in, 1)
            dve.wait_ge(bias_mm, 1)
            link(dve.tensor_copy(act[0:HEADS, 20 * S:21 * S], ps[0:HEADS, 6]))
            dve.tensor_copy(act[0:HEADS, 21 * S:21 * S + P], ps[0:HEADS, 7, 0:P]).then_inc(bias_sb, 1)
            dve.wait_ge(lam_exp, 1)
            link(dve.tensor_tensor(lam[:, 4:5], lam[:, 3:4], lam[:, 2:3], ALU.subtract))
            link(dve.tensor_scalar(lam[:, 6:7], lam[:, 4:5], LAMBDA_INIT, None, ALU.subtract))
            link(dve.tensor_scalar(lam[:, 7:8], pcol("sub_norm_g"), 1.0 - LAMBDA_INIT, None, ALU.mult))
            base = sums_begin(False)
            for c in range(DC):
                sums_add(Step(c), base, chunk(h, c), False)
            rms_apply("conv_norm_g", 0)
            for i in range(2):
                link(dve.memset(conv_in[i][:, 0:CONV - 1], 0.0))
            t0 = stages["pw1"][2]
            a0 = n.take(act_done, DC)
            base = sums_begin(True)
            link.begin(CONV + 1)

            def conv_step(st):
                link.step(st)
                bank = read_tile(st, lambda j: t0 + 2 * j)
                cin = conv_in[st.first % 2]
                dve.wait_ge(act_done, st.at(lambda j: a0 + j + 1))
                link(dve.scalar_tensor_tensor(cin[:, CONV - 1:], bank, pcol_at("conv_b_pw1", st, lambda j: j),
                                              act_tmp[st.first % 2], ALU.add, ALU.mult))
                dve.sem_inc(tile_used, 2)
                y = chunk_at(v_sb, st, lambda j: j)
                for t in range(CONV):
                    tap = pcol_at("conv_dw_w", st, lambda j: j * CONV + t)
                    if t == 0:
                        link(dve.tensor_scalar(y, cin[:, 0:S], tap, pcol_at("conv_dw_b", st, lambda j: j), ALU.mult, ALU.add))
                    else:
                        link(dve.scalar_tensor_tensor(y, cin[:, t:t + S], tap, y, ALU.mult, ALU.add))
                dve.sem_inc(h_ready, 1)
                sums_add(st, base, y, True)

            run_steps(dve, DC, conv_step, 4)
            link.end(DC)
            link.begin(0)
            ln_apply(v_sb, "conv_ln_g", 0)
            residual("pw2", bias="conv_b_pw2")
            for i in range(2):
                rms_apply("ffn_norm_g", i * DC)
                if i == 0:
                    dve.wait_ge(bias_stored, 16)
                    dve.sem_inc(ada_used, 2)
                up_stage(i)
                residual(f"down{i}")
                mod_stage(i)
                rms_apply("ple_norm_g", i * DC)
                ple_stage(i, sums=i == 0)
                if i == 1:
                    break
                rms_apply("attn_norm_g", 0)
                n.take(squared, 2 * DC)
                t0 = stages["qk"][2]
                for j in range(9):
                    if j < 8:
                        for t in (2 * j, 2 * j + 1):
                            dve.tensor_copy(chunk(act, t), one_tile(t0 + t)).then_inc(tile_used, 1)
                    if j >= 1:
                        for t in (2 * j - 2, 2 * j - 1):
                            dve.wait_ge(rinv_done, n.next(rinv_done))
                            dve.scalar_tensor_tensor(chunk(act, t), chunk(act, t), pcol("q_norm_g" if t < 8 else "k_norm_g"),
                                                     rinv[t % 2], ALU.mult, ALU.mult).then_inc(qk_normed, 1)
                t0 = stages["v"][2]
                vv = v_sb[:].rearrange("p (b n) -> p b n", b=NB)
                for t in range(8):
                    dve.tensor_copy(vv[:, 2 * (t % 2):2 * (t % 2) + 2, t // 2 * 256:(t // 2 + 1) * 256],
                                    one_tile(t0 + t).rearrange("p (b n) -> p b n", b=2)).then_inc(tile_used, 1)
                attention("diff")
                residual("wo")

            link.begin(0)
            n.take(xa_ready, DC)
            t0 = stages["e_index"][2]
            for t in range(5):
                link(dve.tensor_copy(chunk(act, E_QI + t), one_tile(t0 + t)))
                dve.sem_inc(tile_used, 1)
            link(dve.tensor_scalar(index_w, one_tile(t0 + 5)[:, 0:32], (HEADS * 64) ** -0.5, None, ALU.mult))
            dve.sem_inc(tile_used, 1)
            dve.sem_inc(index_ready, 1)
            scores = [None] + [chunk(act, E_SC + b - 1) for b in range(1, NB)]
            for b in range(1, NB):
                nk = (b + 1) * P
                sc = scores[b][:, 0:nk]
                for hd in range(HEADS):
                    i = (b - 1) * HEADS + hd
                    dve.wait_ge(relu_done, n.next(relu_done))
                    w_col = index_w[:, b * 8 + hd:b * 8 + hd + 1]
                    if hd == 0:
                        link(dve.tensor_scalar(sc, act_tmp[i % 2][:, 0:nk], w_col, None, ALU.mult))
                    else:
                        link(dve.scalar_tensor_tensor(sc, act_tmp[i % 2][:, 0:nk], w_col, sc, ALU.mult, ALU.add))
                    dve.sem_inc(relu_used, 1)
                link(dve.tensor_tensor(sc[:, nk - P:nk], sc[:, nk - P:nk], chunkmask, ALU.add))
            n.take(scores_ready, 3 * HEADS)
            link(dve.tensor_copy(tables[:, 0:P], chunkmask))
            best = small[:, 32:40]
            rounds = [(b, r) for b in range(1, NB) for r in range(TOPK // 8)]

            def topk_rounds(count):
                for _ in range(min(count, len(rounds))):
                    b, r = rounds.pop(0)
                    nk = (b + 1) * P
                    sc = scores[b][:, 0:nk]
                    link(dve.max(best, sc))
                    link(dve.match_replace(sc, best, sc, TAKEN))
                    if r == TOPK // 8 - 1:
                        m = tables[:, b * S:b * S + nk]
                        link(dve.tensor_scalar(m, sc, TAKEN, 1.0, ALU.is_equal, ALU.subtract))
                        link(dve.tensor_scalar(m, m, -NEG, None, ALU.mult))
                        link(dve.tensor_tensor(m[:, nk - P:nk], m[:, nk - P:nk], chunkmask, ALU.add))

            t0 = stages["e_qk"][2]
            for t in range(8):
                if t < 4:
                    link(dve.tensor_scalar(chunk(act, E_Q + t), one_tile(t0 + t), 64 ** -0.5, None, ALU.mult))
                else:
                    link(dve.tensor_copy(chunk(act, E_K + t - 4), one_tile(t0 + t)))
                dve.sem_inc(tile_used, 1)
                topk_rounds(2)
            t0 = stages["e_v"][2]
            vv = v_sb[:, 0:NB * S].rearrange("p (b n) -> p b n", b=NB)
            for t in range(4):
                link(dve.tensor_copy(vv[:, 2 * (t % 2):2 * (t % 2) + 2, t // 2 * 256:(t // 2 + 1) * 256],
                                     one_tile(t0 + t).rearrange("p (b n) -> p b n", b=2)))
                dve.sem_inc(tile_used, 1)
                topk_rounds(2)
            t0 = stages["e_conv"][2]
            link(dve.memset(e_pad[:, 0:2], 0.0))
            a0 = n.take(act_done, 4)
            for j in range(4):
                bank = one_tile(t0 + 2 * j + 1)
                dve.wait_ge(act_done, a0 + j + 1)
                link(dve.tensor_tensor(e_pad[:, 2:], act_tmp[j % 2], bank, ALU.mult))
                dve.sem_inc(tile_used, 2)
                y = chunk(act, E_CV + j)
                link(dve.tensor_scalar(y, e_pad[:, 0:S], pcol("ev_conv_w", j * 3), None, ALU.mult))
                for t in (1, 2):
                    link(dve.scalar_tensor_tensor(y, e_pad[:, t:t + S], pcol("ev_conv_w", j * 3 + t), y, ALU.mult, ALU.add))
                topk_rounds(4)
            t0 = stages["e_gate"][2]
            for t in range(4):
                y = chunk(act, E_CV + t)
                link(dve.tensor_tensor(y, one_tile(t0 + t), y, ALU.mult))
                dve.sem_inc(tile_used, 1)
                topk_rounds(4)
            topk_rounds(len(rounds))
            dve.sem_inc(even_ready, 1)
            attention("dsa")
            residual("e_out", gate=16)
            ln_apply(h, "ln_mix_g", 0)
            up_conv_stage(2, 0)
            residual("down2", gate=40)
            ln_apply(h, "ln_ffn_g", 0)

            link.begin(0)
            n.take(squared, 5)
            t0 = stages["o_in"][2]
            for g in range(4):
                link(dve.memset(pool_in[g][:, 0:16], 0.0))
                link(dve.tensor_copy(pool_in[g][:, 16:], one_tile(t0 + g)))
                dve.sem_inc(tile_used, 1)
            for i in range(5):
                link(dve.tensor_copy(lat[i], one_tile(t0 + 4 + i)))
                dve.sem_inc(tile_used, 1)
            link(dve.tensor_copy(k_rope_raw[0:QK_DIM], one_tile(t0 + 9)[0:QK_DIM]))
            dve.sem_inc(tile_used, 1)
            dve.sem_inc(rope_raw, 1)
            for i in range(5):
                if i in (0, 3):
                    dve.wait_ge(rinv_done, n.next(rinv_done))
                dve.scalar_tensor_tensor(lat[i], lat[i], pcol("lat_g", i), rinv[0 if i < 3 else 1],
                                         ALU.mult, ALU.mult).then_inc(lat_ready, 1)
            sums_of = [tmp[:, 2 * S:2 * S + POOLW], tmp[:, 6 * S:6 * S + POOLW]]
            first = small[:, 0:16]
            for g, win in enumerate(WINDOWS):
                src, k = pool_in[g], 1
                while k < win:
                    dst = sums_of[(k.bit_length() - 1) % 2]
                    lo = 2 * k - 1
                    link(dve.tensor_tensor(dst[:, lo:], src[:, lo:], src[:, lo - k:POOLW - k], ALU.add))
                    src, k = dst, 2 * k
                x = pool_in[g][:, 16:]
                at = CONST_AT["first_counts"] + g * 16
                link(dve.tensor_tensor(first, src[:, 16:32], con[:, at:at + 16], ALU.mult))
                link(dve.tensor_tensor(first, first, x[:, 0:16], ALU.subtract))
                link(dve.scalar_tensor_tensor(x, src[:, 16:], 1.0 / win, x, ALU.mult, ALU.subtract))
                link(dve.tensor_copy(x[:, 0:16], first))
                dve.sem_inc(pool_ready, 1)
            t0 = stages["o_pool"][2]
            for g in range(4):
                link(dve.tensor_scalar(yc[g], one_tile(t0 + g), pcol("pool_scale", g), None, ALU.mult))
                dve.sem_inc(tile_used, 1)
            rows = slice(NOPE, QK_DIM)
            cos, sin = tables[rows, 3072:3584], tables[rows, 3584:4096]
            turned_part = act_tmp[0][rows]
            dve.wait_ge(rope_mm, 1)
            link(dve.tensor_tensor(turned_part, ps[rows, 6], sin, ALU.mult))
            dve.sem_inc(rope_used, 1)
            link(dve.tensor_tensor(k_rope_raw[rows], k_rope_raw[rows], cos, ALU.mult))
            link(dve.tensor_tensor(k_rope_raw[rows], k_rope_raw[rows], turned_part, ALU.add))
            for g in range(HEADS):
                link(dve.tensor_copy(act[rows, (8 + g) * S:(9 + g) * S], k_rope_raw[rows]))
            t0 = stages["o_uq"][2]
            for j in range(5):
                if j < 4:
                    for hd in (2 * j, 2 * j + 1):
                        link(dve.tensor_scalar(act[0:QK_DIM, hd * S:(hd + 1) * S], one_tile(t0 + hd)[0:QK_DIM], QK_DIM ** -0.5, None, ALU.mult))
                        dve.sem_inc(tile_used, 1)
                        dve.sem_inc(rope_raw, 1)
                if j >= 1:
                    for hd in (2 * j - 2, 2 * j - 1):
                        q = act[rows, hd * S:(hd + 1) * S]
                        dve.wait_ge(rope_mm, hd + 2)
                        link(dve.tensor_tensor(turned_part, ps[rows, 6 + (hd + 1) % 2], sin, ALU.mult))
                        dve.sem_inc(rope_used, 1)
                        link(dve.tensor_tensor(q, q, cos, ALU.mult))
                        link(dve.tensor_tensor(q, q, turned_part, ALU.add))
            t0 = stages["o_ukv"][2]
            for hd in range(HEADS):
                link(dve.tensor_copy(act[0:NOPE, (8 + hd) * S:(9 + hd) * S], one_tile(t0 + hd)[0:NOPE]))
                dve.sem_inc(tile_used, 1)
            for b in range(NB):
                link(dve.tensor_copy(chunk(v_sb, b), one_tile(t0 + HEADS + b)))
                dve.sem_inc(tile_used, 1)
            dve.sem_inc(odd_ready, 1)
            attention("mla")
            residual("o_out", gate=48 + 16)
            ln_apply(h, "ln_mix_g", DC)
            up_conv_stage(3, 1)
            residual("down3", gate=48 + 40)
            ln_apply(h, "ln_ffn_g", DC)

        @block.gpsimd
        def _(pool):
            head = 0
            for kind in ("diff", "dsa", "mla"):
                for g in range(HEADS):
                    head += 1
                    pool.wait_ge(inv_done, head)
                    for b in range(NB):
                        pool.tensor_scalar(probs(g, 0, b), probs(g, 0, b), rowinv[:, b:b + 1], None, ALU.mult).then_inc(scaled, 1)

        @block.scalar
        def _(sc):
            n = Tally()
            link = Chain(sc, a_chain)

            def tile_ready(st, f):
                sc.wait_ge(tile_done, st.at(lambda j: f(j) + 1))
                return ps[:, f(st.first) % BANKS]

            def squares(wait, src, ln, loop=True):
                s0 = n.take(summed, 18 if ln else 9)

                def body(st):
                    wait(st)
                    if loop or st.first >= 2:
                        sc.wait_ge(summed, st.at(lambda j: s0 + (2 * j if ln else j)))
                    sc.activation(sq[st.first % 2], chunk_at(src, st, lambda j: j), ACT.Square).then_inc(squared, 1)

                if loop:
                    run_steps(sc, DC, body, 4)
                else:
                    for c in range(DC):
                        body(Step(c))

            def residual(name, ln):
                t0 = stages[name][2]
                squares(lambda st: sc.wait_ge(tile_used, st.at(lambda j: BANKS + t0 + j + 1)), h, ln)

            def inverse_root(src, scale, eps, to, done=rinv_done, mark=None):
                link(sc.activation(to, src, ACT.Ln, bias=eps, scale=scale))
                if mark is not None:
                    sc.sem_inc(mark, 1)
                sc.activation(to, to, ACT.Exp, scale=-0.5).then_inc(done, 1)

            def rms():
                link.begin(0)
                sc.wait_ge(stat_done, n.next(stat_done))
                inverse_root(ps[:, 4], 1.0 / D, eps_rms, rinv[0])

            def ln(eps, finish):
                link.begin(0)
                sc.wait_ge(stat_done, n.next(stat_done, 2))
                sc.activation(sum1, ps[:, 4], ACT.Copy, scale=1.0 / D).then_inc(mean_done, 1)
                sc.wait_ge(var_done, n.next(var_done))
                inverse_root(sum2, 1.0, eps, rinv[0])
                for c in range(DC):
                    sc.wait_ge(xn_ready, n.next(xn_ready))
                    finish(c, act_tmp[c % 2])

            def to_mixer(c, sh, scl):
                sc.activation(chunk(u, c), chunk(h, c), ACT.Identity, bias=mod[:, sh + c:sh + c + 1],
                              scale=mod[:, scl + c:scl + c + 1]).then_inc(xa_ready, 1)

            def dn_finish(shift_name, at, sh, scl):
                def f(c, xn):
                    hc = chunk(h, c)
                    if sh is None:
                        sc.activation(hc, xn, ACT.Identity, bias=pcol(shift_name, at + c)).then_inc(xa_ready, 1)
                    else:
                        link(sc.activation(hc, xn, ACT.Identity, bias=pcol(shift_name, at + c)))
                        to_mixer(c, sh, scl)
                return f

            def gates(name, func, which, biased=False):
                t0 = stages[name][2]

                def body(st):
                    bank = tile_ready(st, lambda j: t0 + 2 * j + which)
                    sc.wait_ge(tile_used, st.at(lambda j: BANKS + t0 + 2 * j - 2))
                    bias = pcol_at("conv_b_pw1", st, lambda j: DC + j) if biased else con[:, CONST_AT["zero"]:CONST_AT["zero"] + 1]
                    sc.activation(act_tmp[st.first % 2], bank, func, bias=bias).then_inc(act_done, 1)
                return body

            def conv_taps(i, layer):
                t0 = stages[f"up{i}"][2]
                x0 = n.take(x_ready, FC)
                h0 = n.take(h_ready, FC)

                def body(st):
                    for k, (y, at) in enumerate([(act_tmp[st.first % 2], 0), (rinv[st.first % 2], FC)]):
                        bank = tile_ready(st, lambda j: t0 + 2 * j + k)
                        if k == 0:
                            sc.wait_ge(x_ready, st.at(lambda j: x0 + j - 1))
                        tap = pcol_at("ffn_conv_w", st, lambda j: layer * 132 + (at + j) * 3 + 2)
                        sc.activation(y, bank, ACT.Copy, scale=tap).then_inc(act_done, 1)
                    sc.wait_ge(h_ready, st.at(lambda j: h0 + j + 1))
                    y = rinv[st.first % 2]
                    sc.activation(y, y, ACT.Silu).then_inc(act_done, 1)

                run_steps(sc, FC, body, 4)

            def attention(kind):
                link.begin(0)
                G, C, norm = ATT[kind]["heads"], ATT[kind]["comps"], ATT[kind]["norm"]
                t0, o0 = n.take(turned, 4 * G), n.take(o_done, G)
                st0 = n.take(stat_done, G if norm else 0)
                x0 = n.take(x_ready, G if norm else 0)
                for g in range(G + 3):
                    if g < G:
                        if inverses[0] > 0:
                            sc.wait_ge(inv_done, inverses[0])
                        if g >= 2:
                            sc.wait_ge(turned, t0 + 4 * (g - 1))
                        inverses[0] += 1
                        for i in range(4 * C):
                            comp, b = i // 4, i % 4
                            sc.wait_ge(max_done, n.next(max_done))
                            sc.activation(probs(g, comp, b), ps[:, 4 + items[0] % 4, 0:(b + 1) * P], ACT.Exp,
                                          bias=nmax[:, i:i + 1], accum_out=rowsum[:, i:i + 1]).then_inc(exp_done, 1)
                            items[0] += 1
                    if 0 <= g - 1 < G:
                        for kc in (1, 2):
                            sc.wait_ge(turned, t0 + 4 * (g - 1) + kc + 1)
                            if g - 1 >= 2:
                                sc.wait_ge(o_done, o0 + g - 2)
                            sc.activation(probs_t(g - 1, kc), ps[:, kc % 2, 0:(NB - kc) * P], ACT.Copy).then_inc(turned_act, 1)
                    if norm and 0 <= g - 2 < G:
                        sc.wait_ge(o_copied, n.next(o_copied))
                        if g - 2 >= 2:
                            sc.wait_ge(stat_done, st0 + g - 3)
                        sc.activation(sq[g % 2], chunk(u, g - 2), ACT.Square).then_inc(squared, 1)
                    if norm and 0 <= g - 3 < G:
                        sc.wait_ge(stat_done, st0 + g - 2)
                        if g - 3 >= 2:
                            sc.wait_ge(x_ready, x0 + g - 4)
                        inverse_root(ps[:, 3], 1.0 / P, eps_rms, rinv[(g - 3) % 2], mark=ln_done)
                if not norm:
                    n.take(o_copied, G // 2)

            items, inverses = [0], [0]
            sc.wait_ge(inputs_landed, 64)
            sc.activation(cond, par[:, PARAM_AT["c"]:PARAM_AT["c"] + DC], ACT.Silu).then_inc(cond_ready, 1)
            sc.wait_ge(lam_mm, 1)
            sc.activation(lam[:, 2:4], ps[:, 5, 0:2], ACT.Exp).then_inc(lam_exp, 1)
            sc.wait_ge(x_landed, 16 * DC)
            squares(lambda st: None, h, False, loop=False)
            rms()
            n.take(x_ready, DC)
            sigmoid = gates("pw1", ACT.Sigmoid, 1, biased=True)
            s0 = n.take(summed, 18)
            for c in range(DC + 1):
                if c < DC:
                    sigmoid(Step(c))
                if c >= 1:
                    sc.wait_ge(h_ready, n.next(h_ready))
                    sc.wait_ge(summed, s0 + 2 * (c - 1))
                    sc.activation(sq[(c - 1) % 2], chunk(v_sb, c - 1), ACT.Square).then_inc(squared, 1)
            ln(eps_rms, lambda c, xn: sc.activation(chunk(u, c), xn, ACT.Silu, bias=pcol("conv_ln_b", c)).then_inc(xa_ready, 1))
            residual("pw2", False)
            for i in range(2):
                rms()
                n.take(x_ready, DC)
                run_steps(sc, FC, gates(f"up{i}", ACT.Silu, 0), 4)
                n.take(x_ready, FC)
                residual(f"down{i}", False)
                rms()
                n.take(x_ready, DC)
                gate = gates(f"ple{i}", ACT.Sigmoid, 0)
                t0 = stages[f"ple{i}"][2]
                if i == 1:
                    run_steps(sc, DC, gate, 4)
                    break
                s0 = n.take(summed, 9)
                for c in range(DC + 1):
                    if c < DC:
                        gate(Step(c))
                    if c >= 1:
                        sc.wait_ge(tile_used, BANKS + t0 + 2 * c)
                        sc.wait_ge(summed, s0 + c - 1)
                        sc.activation(sq[(c - 1) % 2], chunk(h, c - 1), ACT.Square).then_inc(squared, 1)
                rms()
                n.take(x_ready, DC)
                link.begin(0)
                t0 = stages["qk"][2]
                st0 = n.take(stat_done, 16)
                for j in range(9):
                    if j < 8:
                        for t in (2 * j, 2 * j + 1):
                            sc.wait_ge(tile_used, BANKS + t0 + t + 1)
                            if t >= 2:
                                sc.wait_ge(stat_done, st0 + t - 1)
                            sc.activation(sq[t % 2], chunk(act, t), ACT.Square).then_inc(squared, 1)
                    if j >= 1:
                        for t in (2 * j - 2, 2 * j - 1):
                            sc.wait_ge(stat_done, st0 + t + 1)
                            if t >= 2:
                                sc.wait_ge(qk_normed, t - 1)
                            inverse_root(ps[:, 4 + t % 2], 1.0 / 64, eps_rms, rinv[t % 2], mark=ln_done)
                attention("diff")
                residual("wo", False)
            link.begin(0)
            sc.wait_ge(mod_ready, 2)
            sc.wait_ge(tile_used, BANKS + stages["e_index"][2])
            for c in range(DC):
                to_mixer(c, 0, 8)
            for i in range(3 * HEADS):
                nk = (i // HEADS + 2) * P
                sc.wait_ge(scores_ready, 4 * 2 * HEADS + i + 1)
                if i >= 2:
                    sc.wait_ge(relu_used, i - 1)
                sc.activation(act_tmp[i % 2][:, 0:nk], ps[:, 4 + i % 4, 0:nk], ACT.Relu).then_inc(relu_done, 1)
            sc.wait_ge(relu_used, 3 * HEADS)
            t0 = stages["e_conv"][2]
            for j in range(4):
                bank = tile_ready(Step(0), lambda _: t0 + 2 * j)
                sc.wait_ge(tile_used, BANKS + t0 + 2 * j - 2)
                sc.activation(act_tmp[j % 2], bank, ACT.Copy).then_inc(act_done, 1)
            attention("dsa")
            residual("e_out", True)
            ln(eps_ln, dn_finish("ln_mix_b", 0, 24, 32))
            conv_taps(2, 0)
            residual("down2", True)
            ln(eps_ln, dn_finish("ln_ffn_b", 0, 48, 48 + 8))
            link.begin(0)
            t0 = stages["o_in"][2]
            st0 = n.take(stat_done, 5)
            for i in range(5):
                sc.wait_ge(tile_used, BANKS + t0 + 4 + i + 1)
                if i >= 2:
                    sc.wait_ge(stat_done, st0 + i - 1)
                sc.activation(sq[i % 2], lat[i], ACT.Square).then_inc(squared, 1)
                if i == 2:
                    sc.wait_ge(stat_done, st0 + 3)
                    inverse_root(ps[:, 4], 1.0 / QL, eps_rms, rinv[0])
            sc.wait_ge(stat_done, st0 + 5)
            inverse_root(ps[:, 5], 1.0 / KVL, eps_rms, rinv[1])
            attention("mla")
            residual("o_out", True)
            ln(eps_ln, dn_finish("ln_mix_b", DC, 48 + 24, 48 + 32))
            conv_taps(3, 1)
            residual("down3", True)
            ln(eps_ln, dn_finish("ln_ffn_b", DC, None, None))


def constant_arrays():
    p = np.arange(P)
    ident = np.eye(P, dtype=np.float32)
    ones64 = (p[:, None] // 64 == p[None, :] // 64).astype(np.float32)
    half = ROPE // 2
    rot = np.zeros((P, QK_DIM), np.float32)
    for i in range(half):
        rot[NOPE + half + i, NOPE + i] = -1.0
        rot[NOPE + i, NOPE + half + i] = 1.0
    chunkmask = np.where((p[:, None] < 64) & (p[None, :] >= 64), np.float32(NEG), np.float32(0))
    negdist = -np.abs(p[:, None] - np.arange(S)[None, :] + (S - P)).astype(np.float32)
    counts = np.concatenate([1.0 / np.minimum(np.arange(16) + 1, w) for w in WINDOWS]).astype(np.float32)
    cols = [ident, ident[::-1], np.ones((P, P), np.float32), ones64, rot, chunkmask, negdist,
            np.broadcast_to(counts, (P, 64)), np.full((P, 1), EPS_RMS, np.float32), np.full((P, 1), EPS_LN, np.float32),
            np.zeros((P, 1), np.float32)]
    consts = np.ascontiguousarray(np.concatenate(cols, axis=1), dtype=np.float32)
    slopes = np.concatenate([ident * np.float32(2.0 ** (-8.0 * (i + 1) / HEADS)) for i in range(HEADS)], axis=1)
    inv = np.float32(10000.0) ** (-np.arange(0, ROPE, 2, dtype=np.float32) / np.float32(ROPE))
    ang = np.arange(S, dtype=np.float32)[:, None] * inv[None, :]
    table = lambda f: np.tile(np.tile(f(ang).T.astype(np.float32), (2, 1)), (4, 1))
    late = np.ascontiguousarray(np.concatenate([slopes, table(np.cos), table(np.sin)], axis=1), dtype=np.float32)
    dist = S - 1 - np.arange(640)
    nf = np.maximum(dist, 1).astype(np.float32)
    exact = BUCKETS // 2
    large = exact + (np.log(nf / np.float32(exact)) / np.float32(math.log(128 / exact)) * np.float32(BUCKETS - exact)).astype(np.int32)
    bucket = np.where(dist < exact, np.maximum(dist, 0), np.minimum(large, BUCKETS - 1))
    bucket = np.where(dist < 0, BUCKETS, bucket)
    bucket_of = (np.arange(BUCKETS + 1)[:, None] == bucket[None, :]).astype(np.float32)
    return {"consts": consts, "late": late, "bucket_of": bucket_of}


def kernel(**inputs):
    import concourse.bacc as bacc
    from concourse.bass_utils import run_bass_kernel_spmd

    x = {k: np.asarray(v) for k, v in inputs.items()}

    def feature_columns(v):
        return np.reshape(v, (-1, P)).T

    def taps_last(w):
        return np.reshape(w, (w.shape[0], -1, P)).transpose(2, 1, 0).reshape(P, -1)

    def twice(v):
        return np.concatenate([v.reshape(-1), v.reshape(-1)])[:, None]

    lam = np.zeros((P, 4), np.float32)
    for i, name in enumerate(("q1", "k1", "q2", "k2")):
        lam[0:64, i] = x[f"attn_lambda_{name}"][0]
    packed = {
        "conv_norm_g": feature_columns(x["conv_norm_g"]), "conv_b_pw1": feature_columns(x["conv_b_pw1"]),
        "conv_dw_w": taps_last(x["conv_dw_w"][0]), "conv_dw_b": feature_columns(x["conv_dw_b"]),
        "conv_ln_g": feature_columns(x["conv_ln_g"]), "conv_ln_b": feature_columns(x["conv_ln_b"]),
        "conv_b_pw2": feature_columns(x["conv_b_pw2"]), "attn_norm_g": feature_columns(x["attn_norm_g"]),
        "q_norm_g": twice(x["attn_q_norm_g"]), "k_norm_g": twice(x["attn_k_norm_g"]),
        "sub_norm_g": feature_columns(x["attn_sub_norm_g"]), "lambda": lam,
        "ffn_norm_g": feature_columns(x["ffn_norm_g"]), "ple_norm_g": feature_columns(x["ple_norm_g"]),
        "c": feature_columns(x["c_2"]), "ada_b": feature_columns(x["ada_b_2"]),
        "ln_mix_g": feature_columns(x["ln_mix_g_2"]), "ln_mix_b": feature_columns(x["ln_mix_b_2"]),
        "ln_ffn_g": feature_columns(x["ln_ffn_g_2"]), "ln_ffn_b": feature_columns(x["ln_ffn_b_2"]),
        "ev_conv_w": taps_last(x["ev_conv_w_2"][0]), "pool_scale": feature_columns(x["pool_scale_2"]),
        "lat_g": np.concatenate([feature_columns(x["q_norm_g_2"]), feature_columns(x["kv_norm_g_2"])], axis=1),
        "ffn_conv_w": np.concatenate([taps_last(x["ffn_conv_w_2"][i]) for i in range(2)], axis=1),
    }
    arrays = {
        "params": np.ascontiguousarray(np.concatenate([packed[name] for name, _ in PARAM_WIDTHS], axis=1)),
        "x_t": np.ascontiguousarray(x["x"][0].T), "p_t": np.ascontiguousarray(x["p"][:, 0].transpose(0, 2, 1)),
        "rel_bias": x["rel_bias"],
        "conv_w_pw1": x["conv_w_pw1"][0], "conv_w_pw2": x["conv_w_pw2"][0],
        "attn_w_qkv": x["attn_w_qkv"][0], "attn_w_o": x["attn_w_o"][0],
        "ffn_w_gate": x["ffn_w_gate"], "ffn_w_up": x["ffn_w_up"], "ffn_w_down": x["ffn_w_down"],
        "ple_w_gate": x["ple_w_gate"], "ple_w_proj": x["ple_w_proj"],
        "ada_w": x["ada_w_2"], "ev_w_in": x["ev_w_in_2"][0], "ev_w_out": x["ev_w_out_2"][0],
        "od_w_in": x["od_w_in_2"][0], "pool_w": x["pool_w_2"][0], "w_uq": x["w_uq_2"][0],
        "w_ukv": x["w_ukv_2"][0], "od_w_out": x["od_w_out_2"][0],
        "ffn_w_up2": x["ffn_w_up_2"], "ffn_w_down2": x["ffn_w_down_2"],
        **constant_arrays(),
    }
    nc = bacc.Bacc("TRN2", target_bir_lowering=False, num_devices=1)
    feeds, aps = {}, {}
    for name, v in arrays.items():
        feeds[f"in_{name}"] = np.ascontiguousarray(v)
        aps[name] = nc.dram_tensor(f"in_{name}", v.shape, F32, kind="ExternalInput").ap()
    out = nc.dram_tensor("out_t", (D, S), F32, kind="ExternalOutput").ap()
    build(nc, aps, out)
    result = run_bass_kernel_spmd(nc, [feeds], core_ids=[0])
    return np.ascontiguousarray(result.results[0]["out_t"].T)[None]
```

```python
import math
from contextlib import ExitStack

import concourse.bass as bass
import numpy as np
from concourse import mybir

F32 = mybir.dt.float32
F32R = mybir.dt.float32r
ALU = mybir.AluOpType
ACT = mybir.ActivationFunctionType
AX = mybir.AxisListType

P = 128
S = 512
D = 1024
DC = D // P
NB = S // P
FF = 2816
FC = FF // P
HC = FC // 2
CONV = 31
SIDE = 10
PLE = 256
HEADS = 8
LAMBDA_INIT = 0.8 - 0.6 * math.exp(-0.3)
BUCKETS = 32
DN_ALPHA = 4 ** 0.25
EPS_RMS, EPS_LN = 1e-6, 1e-5
NEG = -1e30
TAKEN = -3e38
TOPK = 128
QL, KVL, ROPE, NOPE = 384, 256, 32, 64
QK_DIM = NOPE + ROPE
WINDOWS = (2, 4, 8, 16)
RING = 4
HI_RING = 2
BANKS = 4
SLOT = 2048

PARAM_WIDTHS = [
    ("conv_norm_g", 8), ("conv_b_pw1", 16), ("conv_dw_w", 8 * CONV), ("conv_dw_b", 8),
    ("conv_ln_g", 8), ("conv_ln_b", 8), ("conv_b_pw2", 8), ("attn_norm_g", 8),
    ("q_norm_g", 1), ("k_norm_g", 1), ("sub_norm_g", 1), ("lambda", 4),
    ("ffn_norm_g", 16), ("ple_norm_g", 16), ("c", 8), ("ada_b", 96),
    ("ln_mix_g", 16), ("ln_mix_b", 16), ("ln_ffn_g", 16), ("ln_ffn_b", 16),
    ("ev_conv_w", 12), ("pool_scale", 4), ("lat_g", 5), ("ffn_conv_w", 2 * 3 * 44),
]
PARAM_AT, _n = {}, 0
for _name, _w in PARAM_WIDTHS:
    PARAM_AT[_name] = _n
    _n += _w
N_PARAMS = _n

CONST_WIDTHS = [("ident", P), ("flip", P), ("ones", P), ("ones64", P), ("rot", QK_DIM), ("key_rot", QK_DIM), ("key_move", QK_DIM), ("chunkmask", P),
                ("negdist", S), ("first_counts", 64), ("eps", 2), ("zero", 1)]
CONST_AT, _n = {}, 0
for _name, _w in CONST_WIDTHS:
    CONST_AT[_name] = _n
    _n += _w
N_CONSTS = _n
LATE_WIDTH = HEADS * P + 2 * S


WIDTHS = {"ple0": 10 * P, "ple1": 10 * P, "e_keyw": DC * 136}
UNSPLIT = ("o_pool", "o_uq", "o_ukv")


def plan_slots():
    stages, loads, tiles_after, split_no, width = {}, [], [], [], []
    tiles = splits = 0

    def stage(name, slots, tiles_of_slot, transfers=1):
        nonlocal tiles, splits
        stages[name] = (len(loads), slots, tiles)
        for j in range(slots):
            loads.append(transfers)
            tiles += tiles_of_slot
            tiles_after.append(tiles)
            splits += name not in UNSPLIT
            split_no.append(0 if name in UNSPLIT else splits)
            down = name.startswith("down")
            width.append(HC * P if down else DC * 160 if (name, j) == ("o_in", 4) else WIDTHS.get(name, SLOT))

    def ffn(n):
        for part in "ab":
            stage(f"up{n}{part}", HC, 2, 2)
            stage(f"down{n}{part}", DC, 1)

    stage("pw1", DC, 2, 2)
    stage("pw2", 4, 2)
    ffn(0)
    stage("ple0", DC, 2, 2)
    stage("qk", 8, 2)
    stage("v", 4, 2)
    stage("wo", 4, 2)
    ffn(1)
    stage("ple1", DC, 2, 2)
    stage("e_index", 2, 2)
    stage("e_keyw", 1, 2, 3)
    stage("e_qk", 4, 2)
    stage("e_v", 2, 2)
    stage("e_conv", 4, 2, 2)
    stage("e_gate", 2, 2)
    stage("e_out", 4, 2)
    ffn(2)
    stage("o_in", 5, 2)
    stage("o_uq", 4, 2)
    stage("o_pool", 1, 4)
    stage("o_ukv", 1, 12)
    stage("o_out", 4, 2)
    ffn(3)
    so_far, landed_due = [0] * RING, []
    for k, n in enumerate(loads):
        so_far[k % RING] += 16 * n
        landed_due.append(so_far[k % RING])
    return stages, landed_due, tiles_after, split_no, width


class Step:

    def __init__(self, first, counter=None, unroll=0):
        self.first, self.counter, self.unroll = first, counter, unroll

    def at(self, f):
        if self.counter is None:
            return f(self.first)
        return f(self.first) + self.counter * (f(self.first + self.unroll) - f(self.first))


def run_steps(engine, n, body, unroll=4, peel=0, tail=0):
    for j in range(min(peel, n)):
        body(Step(j))
    turns = (n - peel - tail) // unroll
    if turns > 1:
        with engine.Fori(0, turns) as i:
            for s in range(unroll):
                body(Step(peel + s, i, unroll))
    else:
        turns = 0
    for j in range(peel + turns * unroll, n):
        body(Step(j))


class Tally:

    def __init__(self):
        self.seen = {}

    def next(self, sem, n=1):
        self.seen[sem.name] = self.seen.get(sem.name, 0) + n
        return self.seen[sem.name]

    def take(self, sem, n):
        return self.next(sem, n) - n


class Chain:

    def __init__(self, engine, sem):
        self.engine, self.sem = engine, sem
        self.base = self.local = 0
        self.per, self.step_base = 0, 0

    def begin(self, per):
        self.base += self.local
        self.local, self.per = 0, per

    def step(self, st):
        assert self.local in (0, self.per), self.local
        self.local = 0
        self.step_base = st.at(lambda j: j * self.per)

    def end(self, n):
        assert self.local == self.per, self.local
        self.base += n * self.per
        self.local = self.step_base = 0

    def __call__(self, instruction, open_=0):
        instruction.then_inc(self.sem, 1)
        self.local += 1
        self.engine.wait_ge(self.sem, self.base + self.step_base + self.local - open_)


def build(nc, a, out):
    stages, landed_due, tiles_after, split_no, slot_width = plan_slots()
    n_slots = len(slot_width)
    with ExitStack() as ctx:
        place = [-(-nc.sbuf_base // 32) * 32]

        def region(floats, *tensors):
            made = [nc.alloc_sbuf_tensor_at(name, [P, n_], dt, offset=place[0] + 4 * at) for name, at, n_, dt in tensors]
            place[0] += -(-4 * floats // 32) * 32
            return made if len(made) > 1 else made[0]

        def sb(name, width, dt=F32):
            return region(width, (name, 0, width, dt))

        def sem(name):
            return ctx.enter_context(nc.semaphore(name))

        pairs = [region(SLOT, (f"weight_raw{s}", 0, SLOT, F32), (f"weight_lo{s}", 0, SLOT, F32R)) for s in range(RING)]
        raw, w_lo = [r for r, _ in pairs], [l for _, l in pairs]
        w_hi = [sb(f"weight_hi{s}", SLOT, F32R) for s in range(HI_RING)]
        h = sb("h", DC * S)
        u_hi, u_lo = sb("u_hi", DC * S, F32R), sb("u_lo", DC * S, F32R)
        act, act_hi, act_lo = region(FC * S, ("act", 0, FC * S, F32), ("act_hi", 0, HC * S, F32R),
                                     ("act_lo", HC * S, HC * S, F32R))
        arena = sb("arena", 8192)
        tmp = sb("tmp", 8 * S)
        par = sb("par", N_PARAMS)
        con = sb("con", N_CONSTS)
        p_sb, p_lo, p_hi = region(4 * S, ("p_sb", 0, 4 * S, F32), ("p_lo", 0, 2 * S, F32R), ("p_hi", 2 * S, 2 * S, F32R))
        mod = sb("mod", 96)
        small = sb("small", 64)
        ps = ctx.enter_context(nc.psum_tensor("ps", [P, 8, S], F32))
        bias_rows = nc.dram_tensor("bias_rows", [HEADS, 640], F32).ap()

        def chunk(t, c, n=1):
            return t[:, c * S:(c + n) * S]

        def pcol(name, i=0):
            at = PARAM_AT[name] + i
            return par[:, at:at + 1]

        def pcol_at(name, st, f):
            if st.counter is None:
                return pcol(name, f(st.first))
            return par[:, bass.ds(st.at(lambda j: PARAM_AT[name] + f(j)), 1)]

        def chunk_at(t, st, f):
            if st.counter is None:
                return chunk(t, f(st.first))
            return t[:, bass.ds(st.at(lambda j: f(j) * S), S)]

        def const(name, width=None):
            at = CONST_AT[name]
            return con[:, at:at + (width or dict(CONST_WIDTHS)[name])]

        ident, flip, ones, ones64 = const("ident"), const("flip"), const("ones"), const("ones64")
        rot, chunkmask, negdist = const("rot"), const("chunkmask"), const("negdist")
        key_rot, key_move = const("key_rot"), const("key_move")
        eps_rms, eps_ln = con[:, CONST_AT["eps"]:CONST_AT["eps"] + 1], con[:, CONST_AT["eps"] + 1:CONST_AT["eps"] + 2]
        sq = [chunk(tmp, 0), chunk(tmp, 1)]
        sum1, sum2 = chunk(tmp, 2), chunk(tmp, 3)
        rinv = [chunk(tmp, 4), chunk(tmp, 5)]
        act_tmp = [chunk(tmp, 6), chunk(tmp, 7)]
        ada_acc = arena[:, 0:6 * D]
        ada_slot = [arena[:, (6 + s) * D:(7 + s) * D] for s in range(2)]
        conv_out = arena[:, 0:DC * S]
        WP = sum((b + 1) * P for b in range(NB))
        p_off = [sum((x + 1) * P for x in range(b)) for b in range(NB)]
        v_sb = arena[:, 0:4096]
        bias_tab = [arena[:, 4096 + s * S:4096 + (s + 1) * S] for s in range(2)]
        masks = arena[:, 2048:4096]
        slopes = arena[:, 4096:5120]
        rope_tab = arena[:, 2048:3072]
        MAPS = {
            "diff": [arena[:, 5120:5120 + 2 * WP], act[:, 16 * S:16 * S + 2 * WP]],
            "dsa": [arena[:, 5120:5120 + WP], arena[:, 5120 + WP:5120 + 2 * WP]],
            "mla": [arena[:, 5632:5632 + WP], arena[:, 5632 + WP:5632 + 2 * WP]],
        }

        def cut(t, at, n_):
            return t[:, at:at + n_]

        pt_even = [cut(p_sb, 0, 512), cut(p_sb, 512, 384), cut(p_sb, 896, 256), cut(p_sb, 1152, 128)]
        pt_rest = [cut(p_sb, 1280, 384), cut(p_sb, 1664, 256), cut(p_sb, 1920, 128)]
        TURNED = {
            "diff": [pt_even, [cut(act, 21 * S, 512), cut(arena, 7680, 384), cut(tmp, 2 * S, 256), cut(arena, 8064, 128)]],
            "dsa": [pt_even, [cut(arena, 7680, 512)] + pt_rest],
            "mla": [pt_even, [cut(arena, 3072, 512)] + pt_rest],
        }

        def probs(kind, g, comp, b):
            at = comp * WP + p_off[b]
            return MAPS[kind][g % 2][:, at:at + (b + 1) * P]

        def probs_t(kind, g, kc):
            return TURNED[kind][g % 2][kc]

        PADW = CONV - 1 + S
        conv_in = [act[:, i * PADW:(i + 1) * PADW] for i in range(2)]
        conv_odd = act[:, 2 * PADW:2 * PADW + S]
        side_at = 2 * PADW + S
        side_acc = [act[:, side_at + i * S:side_at + (i + 1) * S] for i in range(2)]
        side_prod = [act[:, side_at + i * S:side_at + (i + 1) * S] for i in range(2, 5)]
        E_Q, E_K, E_QI, E_KI, E_CV, E_SC = 0, 4, 8, 12, 13, 17
        e_pad = act[:, 20 * S:20 * S + 2 + S]
        index_w = small[:, 0:32]
        index_raw = rinv[0]
        POOLW = 16 + S
        pool_in = [act[:, 16 * S + g * POOLW:16 * S + (g + 1) * POOLW] for g in range(4)]
        lat = [arena[:, 3072 + i * S:3072 + (i + 1) * S] for i in range(5)]
        k_rope_raw = act[:, 16 * S + 4 * POOLW:17 * S + 4 * POOLW]
        nmax = small[:, 32:40]
        rowsum = small[:, 40:48]
        rowinv = small[:, 48:56]
        lam = small[:, 56:64]
        cond = small[:, 0:8]

        landed = [sem(f"weights_landed{s}") for s in range(RING)]
        ada_landed = [sem(f"ada_landed{s}") for s in range(2)]
        inputs_landed = sem("inputs_landed")
        x_landed = sem("x_landed")
        p_landed = sem("p_landed")
        bias_landed = [sem(f"bias_landed{s}") for s in range(2)]
        tables_landed = sem("tables_landed")
        bias_stored = sem("bias_stored")
        out_stored = sem("out_stored")
        tile_done = sem("tile_done")
        tile_used = sem("tile_used")
        h_ready = sem("h_ready")
        squared = sem("squared")
        summed = sem("summed")
        stat_done = sem("stat_done")
        mean_done = sem("mean_done")
        even_ready, odd_ready, index_ready = sem("even_ready"), sem("odd_ready"), sem("index_ready")
        index_copied, index_turned = sem("index_copied"), sem("index_turned")
        lat_ready = sem("lat_ready")
        rope_used = sem("rope_used")
        rope_raw = sem("rope_raw")
        var_done = sem("var_done")
        rinv_done = sem("rinv_done")
        t_ready = sem("t_ready")
        hi_done = sem("hi_done")
        x_ready = sem("x_ready")
        w_rounded = sem("w_rounded")
        w_ready = sem("w_ready")
        p_rounded, p_ready = sem("p_rounded"), sem("p_ready")
        h_out = sem("h_out")
        conv_in_ready = sem("conv_in_ready")
        side_ready = sem("side_ready")
        side_added = sem("side_added")
        side_used = sem("side_used")
        xn_ready = sem("xn_ready")
        act_done = sem("act_done")
        ada_used = sem("ada_used")
        ada_summed = sem("ada_summed")
        mod_done = sem("mod_done")
        mod_ready = sem("mod_ready")
        cond_ready = sem("cond_ready")
        d_chain, a_chain = sem("d_chain"), sem("a_chain")
        qk_normed = sem("qk_normed")
        ln_done = sem("ln_done")
        bias_in = sem("bias_in")
        bias_mm = sem("bias_mm")
        bias_sb = sem("bias_sb")
        lam_in = sem("lam_in")
        lam_mm = sem("lam_mm")
        lam_exp = sem("lam_exp")
        scores_ready = sem("scores_ready")
        max_done = sem("max_done")
        exp_done = sem("exp_done")
        inv_done = sem("inv_done")
        scaled = sem("scaled")
        mixed = sem("mixed")
        turned = sem("turned")
        turned_dve, turned_act = sem("turned_dve"), sem("turned_act")
        o_done = sem("o_done")
        o_copied = sem("o_copied")
        relu_done = sem("relu_done")
        relu_used = sem("relu_used")
        rope_mm = sem("rope_mm")
        pool_ready = sem("pool_ready")

        def q_chunk(c):
            return chunk(act, c)

        def head_rows(h_, width):
            return slice(64 * (h_ % 2), 64 * (h_ % 2) + 64)

        def tok(b):
            return slice(b * P, (b + 1) * P)

        ATT = {
            "diff": dict(heads=HEADS, comps=2, norm=True),
            "dsa": dict(heads=HEADS, comps=1, norm=False),
            "mla": dict(heads=HEADS, comps=1, norm=False),
        }

        block = ctx.enter_context(nc.Block())

        @block.sync
        def _(sp):
            n = Tally()
            sp.dma_start(par[:], a["params"]).then_inc(inputs_landed, 16)
            sp.dma_start(con[:], a["consts"]).then_inc(inputs_landed, 16)
            for c in range(DC):
                sp.dma_start(chunk(h, c), a["x_t"][c * P:(c + 1) * P]).then_inc(x_landed, 16)
            sp.dma_start(v_sb[0:BUCKETS, 0:HEADS], a["rel_bias"]).then_inc(inputs_landed, 16)
            sp.dma_start(v_sb[0:BUCKETS + 1, 8:648], a["bucket_of"]).then_inc(inputs_landed, 16)

            def load(name, sources, unroll=4):
                k0, slots, _ = stages[name]

                def body(st):
                    s = (k0 + st.first) % RING
                    if k0 + st.first >= RING:
                        sp.wait_ge(tile_done, st.at(lambda j: tiles_after[k0 + j - RING]))
                    for dst, src in sources(st, raw[s]):
                        sp.dma_start(dst, src).then_inc(landed[s], 16)

                run_steps(sp, slots, body, unroll, peel=4)

            def columns(w, st, f, width=256):
                w = w.rearrange("(c p) n -> p c n", p=P)
                if st.counter is None:
                    return w[:, :, f(st.first):f(st.first) + width]
                return w[:, :, bass.ds(st.at(f), width)]

            def k_by(slot, kc, width):
                return slot[:, 0:kc * width].rearrange("p (c n) -> p c n", c=kc)

            def plain(w, at=0, kc=DC, width=256):
                return lambda st, slot: [(k_by(slot, kc, width), columns(w, st, lambda j: at + j * width, width))]

            def pair(wa, wb, at_a=0, at_b=0, kb=DC):
                def f(st, slot):
                    return [
                        (k_by(slot[:, 0:DC * P], DC, P), columns(wa, st, lambda j: at_a + j * P, P)),
                        (k_by(slot[:, DC * P:], kb, P), columns(wb, st, lambda j: at_b + j * P, P)),
                    ]
                return f

            def ffn(i, gate, up, dn, at_b=0):
                for z, part in enumerate("ab"):
                    first = z * HC * P
                    load(f"up{i}{part}", pair(gate, up, first, at_b + first))
                    load(f"down{i}{part}", plain(dn[first:first + HC * P], 0, HC, P))

            load("pw1", pair(a["conv_w_pw1"], a["conv_w_pw1"], 0, D))
            sp.wait_ge(bias_sb, 1)
            sp.dma_start(bias_rows, act[0:HEADS, 20 * S:20 * S + 640]).then_inc(bias_stored, 16)
            load("pw2", plain(a["conv_w_pw2"]))
            ffn(0, a["ffn_w_gate"][0], a["ffn_w_up"][0], a["ffn_w_down"][0])
            sp.dma_start(p_sb[:, 0:2 * S].rearrange("p (c n) -> p c n", c=2), a["p_t"][0].rearrange("(c p) n -> p c n", p=P)).then_inc(p_landed, 16)
            load("ple0", pair(a["ple_w_gate"][0], a["ple_w_proj"][0], kb=2))
            load("qk", plain(a["attn_w_qkv"]))
            load("v", plain(a["attn_w_qkv"], 2 * D))
            load("wo", plain(a["attn_w_o"]))
            sp.wait_ge(bias_stored, 16)
            sp.wait_ge(mod_ready, n.next(mod_ready))
            for hd in range(HEADS):
                if hd >= 2:
                    sp.wait_ge(scores_ready, 2 * NB * (hd - 1))
                sp.dma_start(bias_tab[hd % 2], bass.AP(bias_rows.tensor, hd * 640, [[1, P], [1, S]])).then_inc(bias_landed[hd % 2], 16)
            sp.wait_ge(tile_done, stages["wo"][2] + 1)
            sp.dma_start(p_sb[:, 0:2 * S].rearrange("p (c n) -> p c n", c=2), a["p_t"][1].rearrange("(c p) n -> p c n", p=P)).then_inc(p_landed, 16)
            ffn(1, a["ffn_w_gate"][1], a["ffn_w_up"][1], a["ffn_w_down"][1])
            load("ple1", pair(a["ple_w_gate"][1], a["ple_w_proj"][1], kb=2))
            w = a["ev_w_in"]
            load("e_index", plain(w, 1536))

            def key_and_w(st, slot):
                to = slot[:, 0:DC * 136].rearrange("p (c n) -> p c n", c=DC)
                wr = w.rearrange("(c p) n -> p c n", p=P)
                return [(to[:, :, 0:64], wr[:, :, 2048:2112]), (to[:, :, 64:128], wr[:, :, 2048:2112]),
                        (to[:, :, 128:136], wr[:, :, 2112:2120])]

            load("e_keyw", key_and_w)
            sp.wait_ge(mod_ready, n.next(mod_ready))
            sp.dma_start(slopes, a["late"][:, 0:HEADS * P]).then_inc(tables_landed, 16)
            load("e_qk", plain(w, 0))
            load("e_v", plain(w, 1024))
            load("e_conv", pair(w, w, 2632, 3144))
            load("e_gate", plain(w, 2120))
            load("e_out", plain(a["ev_w_out"]))
            sp.wait_ge(tile_done, stages["e_out"][2] + 1)
            sp.dma_start(rope_tab, a["late"][:, HEADS * P:]).then_inc(tables_landed, 16)
            ffn(2, a["ffn_w_up2"][0], a["ffn_w_up2"][0], a["ffn_w_down2"][0], at_b=FF)
            w2 = a["od_w_in"].rearrange("(c p) n -> p c n", p=P)

            def odd_in(st, slot):
                width = 256 if st.first < 4 else 160
                return [(k_by(slot, DC, width), w2[:, :, st.first * 256:st.first * 256 + width])]

            load("o_in", odd_in, unroll=8)
            load("o_uq", plain(a["w_uq"], 0, 3, 192))
            load("o_pool", lambda st, slot: [(k_by(slot, 4, P), a["pool_w"].rearrange("g c d -> c g d"))])
            load("o_ukv", lambda st, slot: [(k_by(slot, 2, D), a["w_ukv"].rearrange("(c p) n -> p c n", p=P))])
            load("o_out", plain(a["od_w_out"]))
            ffn(3, a["ffn_w_up2"][1], a["ffn_w_up2"][1], a["ffn_w_down2"][1], at_b=FF)
            for c in range(DC):
                sp.wait_ge(h_out, c + 1)
                sp.dma_start(out[c * P:(c + 1) * P], chunk(h, c)).then_inc(out_stored, 16)
            sp.wait_ge(out_stored, 16 * DC)

        @block.tensor
        def _(pe):
            n = Tally()
            pe.sem_inc(tile_used, BANKS)
            pe.wait_ge(inputs_landed, 64)

            def slot_of(name, st):
                k0 = stages[name][0]
                k = k0 + st.first
                pe.wait_ge(w_ready, st.at(lambda j: split_no[k0 + j]))
                return w_hi[k % HI_RING], w_lo[k % RING]

            def raw_slot(name, j=0):
                k = stages[name][0] + j
                pe.wait_ge(landed[k % RING], landed_due[k])
                return raw[k % RING]

            def open_tile(t0, st, per, i):
                t = lambda j: t0 + per * j + i
                pe.wait_ge(tile_used, st.at(lambda j: t(j) + 1))
                return ps[:, t(st.first) % BANKS]

            def product(bank, w, x, start, stop):
                pe.matmul(bank, w[0], x[0], start=start, stop=False)
                pe.matmul(bank, w[0], x[1], start=False, stop=False)
                return pe.matmul(bank, w[1], x[0], start=False, stop=stop)

            def halves(pair_, f):
                return f(pair_[0]), f(pair_[1])

            def xu(k):
                return chunk(u_hi, k), chunk(u_lo, k)

            def plain_cols(w, i, k):
                return halves(w, lambda t: t[:, k * 256 + i * P:k * 256 + (i + 1) * P])

            def pair_cols(w, i, k):
                return halves(w, lambda t: t[:, i * DC * P + k * P:i * DC * P + (k + 1) * P])

            PLAIN = ("pw2", "qk", "wo", "e_index", "e_qk", "e_gate", "e_out", "o_in", "o_out")

            def stage_gemm(name, x=(xu, xu), kc=(DC, DC), wait=True, behind=None, order=range(DC)):
                t0 = stages[name][2]
                cols = plain_cols if name in PLAIN else pair_cols

                def body(st):
                    w = slot_of(name, st)
                    for i in range(2):
                        bank = open_tile(t0, st, 2, i)
                        for k in range(kc[i]):
                            mm = product(bank, cols(w, i, k), x[i](k), k == 0, k == kc[i] - 1)
                        mm.then_inc(tile_done, 1)
                    if behind:
                        behind(st.first)

                if not wait:
                    run_steps(pe, stages[name][1], body, 4)
                    return
                for k in order:
                    pe.wait_ge(x_ready, n.next(x_ready))
                    if k == order[0]:
                        w = slot_of(name, Step(0))
                        banks = [open_tile(t0, Step(0), 2, i) for i in range(2)]
                    for i in range(2):
                        if k < kc[i]:
                            mm = product(banks[i], cols(w, i, k), x[i](k), k == order[0], k == (order[-1] if kc[i] == DC else kc[i] - 1))
                            if k == order[-1]:
                                mm.then_inc(tile_done, 1 if kc[1] == DC else 2)
                if behind:
                    behind(0)

                rest(name, body, stages[name][1] - 1)

            def rest(name, body, count):
                turns = count // 4
                if turns > 1:
                    with pe.Fori(0, turns) as i:
                        for s in range(4):
                            body(Step(1 + s, i, 4))
                else:
                    turns = 0
                for j in range(1 + 4 * turns, 1 + count):
                    body(Step(j))

            def stage_down(name):
                t0 = stages[name][2]
                x0 = n.take(x_ready, HC)

                def body(st):
                    w = slot_of(name, st)
                    bank = open_tile(t0, st, 1, 0)
                    for k in range(HC):
                        if k in (0, HC - 1):
                            pe.wait_ge(x_ready, x0 + (HC - 1 if k == 0 else HC))
                        mm = product(bank, halves(w, lambda t: t[:, k * P:(k + 1) * P]),
                                     (chunk(act_hi, k), chunk(act_lo, k)), k == 0, k == HC - 1)
                    mm.then_inc(tile_done, 1)

                run_steps(pe, DC, body, 4)

            def rms_stat(adds=9):
                n.take(squared, DC)
                pe.wait_ge(summed, n.next(summed, adds))
                pe.matmul(ps[:, 4], ones, sum2, start=True, stop=True).then_inc(stat_done, 1)

            def ln_stat():
                n.take(squared, DC)
                pe.wait_ge(summed, n.next(summed, 18))
                pe.matmul(ps[:, 4], ones, sum1, start=True, stop=True).then_inc(stat_done, 1)
                pe.matmul(ps[:, 5], ones, sum2, start=True, stop=True).then_inc(stat_done, 1)

            def mod_vector(half):
                if half == 0:
                    pe.wait_ge(ada_summed, n.next(ada_summed))
                for c in range(24 * half, 24 * half + 24):
                    mm = pe.matmul(ps[:, 6, c:c + 1], ada_acc[:, c * P:(c + 1) * P], ones[:, 0:1], start=True, stop=True)
                if half:
                    mm.then_inc(mod_done, 1)

            def values(name):
                t0 = stages[name][2]

                def body(st):
                    w = slot_of(name, st)
                    for i in range(2):
                        bank = open_tile(t0, st, 2, i)
                        for b in range(2):
                            for k in range(DC):
                                mm = product(bank[:, b * 256:(b + 1) * 256],
                                             halves(xu(k), lambda t: t[:, tok(2 * i + b)]),
                                             halves(w, lambda t: t[:, k * 256:(k + 1) * 256]), k == 0, k == DC - 1)
                        mm.then_inc(tile_done, 1)

                run_steps(pe, stages[name][1], body, 4)

            def attention(kind):
                spec = ATT[kind]
                G, C = spec["heads"], spec["comps"]
                item = 0
                pe.wait_ge(tile_used, {"diff": stages["wo"][2], "dsa": stages["e_out"][2], "mla": stages["o_out"][2]}[kind] + BANKS)

                def score_tiles(g):
                    nonlocal item
                    for comp in range(C):
                        for b in range(NB):
                            nk = (b + 1) * P
                            if item >= 4:
                                pe.wait_ge(exp_done, n.next(exp_done))
                            bank = ps[:, 4 + item % 4, 0:nk]
                            at = 384 - b * P
                            if kind == "diff":
                                r = slice(64 * comp, 64 * comp + 64)
                                pe.matmul(bank, q_chunk(g)[r, tok(b)], q_chunk(8 + g)[r, 0:nk], start=True, stop=False)
                                pe.wait_ge(bias_landed[g % 2], 16 * (g // 2 + 1))
                                mm = pe.matmul(bank, flip, bias_tab[g % 2][:, at:at + nk], start=False, stop=True)
                            elif kind == "dsa":
                                r = slice(64 * (g % 2), 64 * (g % 2) + 64)
                                pe.matmul(bank, q_chunk(E_Q + g // 2)[r, tok(b)], q_chunk(E_K + g // 2)[r, 0:nk], start=True, stop=False)
                                pe.matmul(bank, slopes[:, g * P:(g + 1) * P], negdist[:, at:at + nk], start=False, stop=False)
                                mm = pe.matmul(bank, ident, masks[:, b * S:b * S + nk], start=False, stop=True)
                            else:
                                pe.matmul(bank, act[0:QK_DIM, g * S + b * P:g * S + (b + 1) * P],
                                          act[0:QK_DIM, (8 + g) * S:(8 + g) * S + nk], start=True, stop=False)
                                mm = pe.matmul(ps[:, 4 + item % 4, nk - P:nk], ident, chunkmask, start=False, stop=True)
                            mm.then_inc(scores_ready, 1)
                            item += 1

                def turn(g, chunks):
                    if chunks[0] == 0:
                        if kind == "diff":
                            n.take(scaled, 4)
                            pe.wait_ge(mixed, n.next(mixed, 4))
                        else:
                            pe.wait_ge(scaled, n.next(scaled, 4))
                    for kc in chunks:
                        if g > 0 or kc >= 2:
                            copied = (turned_act, turned_dve, turned_dve, turned_act)[kc]
                            pe.wait_ge(copied, turned_at + 2 * g + kc // 2)
                        for b in range(kc, NB):
                            mm = pe.transpose(ps[:, kc % 2, (b - kc) * P:(b - kc + 1) * P],
                                              probs(kind, g, 0, b)[:, kc * P:(kc + 1) * P], ident)
                        mm.then_inc(turned, 1)

                def weigh(g):
                    pe.wait_ge(turned_dve, 2 * (g + 1) + turned_at)
                    pe.wait_ge(turned_act, 2 * (g + 1) + turned_at)
                    dim = P if kind == "diff" else 64
                    r0 = 0 if kind == "diff" else 64 * (g % 2)
                    if kind == "diff" or g % 2 == 0:
                        if g > 0:
                            pe.wait_ge(o_copied, n.next(o_copied))
                    for kc in range(NB):
                        if kind == "diff":
                            val = v_sb[:, kc * D + g * P:kc * D + (g + 1) * P]
                        else:
                            val = v_sb[:, kc * S + g * 64:kc * S + (g + 1) * 64]
                        mm = pe.matmul(ps[r0:r0 + dim, 2, kc * P:S], val, probs_t(kind, g, kc), start=kc == 0, stop=kc == NB - 1)
                    mm.then_inc(o_done, 1)

                def stat(g):
                    pe.wait_ge(squared, n.next(squared))
                    if g > 0:
                        pe.wait_ge(ln_done, n.next(ln_done))
                    pe.matmul(ps[:, 3], ones, sq[g % 2], start=True, stop=True).then_inc(stat_done, 1)

                turned_at = 2 * HEADS * {"diff": 0, "dsa": 1, "mla": 2}[kind]
                for g in range(G + 3):
                    if g < G:
                        score_tiles(g)
                    if 0 <= g - 1 < G:
                        turn(g - 1, (0, 1))
                    if 0 <= g - 2 < G:
                        weigh(g - 2)
                    if 0 <= g - 1 < G:
                        turn(g - 1, (2, 3))
                    if spec["norm"] and 0 <= g - 3 < G:
                        stat(g - 3)
                pe.wait_ge(o_copied, n.next(o_copied))
                n.next(exp_done, 4)
                if spec["norm"]:
                    n.next(ln_done)

            pe.wait_ge(bias_in, n.next(bias_in))
            pe.matmul(ps[0:HEADS, 6], v_sb[0:BUCKETS + 1, 0:HEADS], v_sb[0:BUCKETS + 1, 8:520], start=True, stop=True)
            pe.matmul(ps[0:HEADS, 7, 0:P], v_sb[0:BUCKETS + 1, 0:HEADS], v_sb[0:BUCKETS + 1, 520:648], start=True, stop=True).then_inc(bias_mm, 1)
            pe.wait_ge(lam_in, 1)
            pe.matmul(ps[:, 5, 0:2], ones[0:64, :], lam[0:64, 0:2], start=True, stop=True).then_inc(lam_mm, 1)
            rms_stat()
            stage_gemm("pw1")
            ln_stat()
            stage_gemm("pw2")
            for i in range(2):
                rms_stat()
                for part in "ab":
                    stage_gemm(f"up{i}{part}", wait=part == "a")
                    stage_down(f"down{i}{part}")
                rms_stat()
                mod_vector(0)
                pe.wait_ge(p_ready, i + 1)
                stage_gemm(f"ple{i}", (xu, lambda k: (chunk(p_hi, k), chunk(p_lo, k))), kc=(DC, 2))
                if i:
                    mod_vector(1)
                    break
                rms_stat()
                mod_vector(1)

                def head_sums(j):
                    for t in (2 * j, 2 * j + 1):
                        pe.wait_ge(squared, n.next(squared))
                        if t >= 2:
                            pe.wait_ge(ln_done, n.next(ln_done))
                        pe.matmul(ps[:, 4 + t % 2], ones64, sq[t % 2], start=True, stop=True).then_inc(stat_done, 1)

                stage_gemm("qk", behind=lambda j: head_sums(j - 1) if j >= 1 else None)
                head_sums(7)
                n.next(ln_done, 2)
                values("v")
                pe.wait_ge(qk_normed, 16)
                attention("diff")
                stage_gemm("wo")
            stage_gemm("e_index")
            t0 = stages["e_keyw"][2]
            w = slot_of("e_keyw", Step(0))
            bank = open_tile(t0, Step(0), 2, 0)
            for k in range(DC):
                mm = product(bank, halves(w, lambda t: t[:, k * 136:k * 136 + P]), xu(k), k == 0, k == DC - 1)
            mm.then_inc(tile_done, 1)
            bank = open_tile(t0, Step(0), 2, 1)
            for k in range(DC):
                mm = product(bank, halves(w, lambda t: t[:, k * 136 + 8:(k + 1) * 136]), xu(k), k == 0, k == DC - 1)
            mm.then_inc(tile_done, 1)
            pe.wait_ge(index_copied, 1)
            for b in range(NB):
                mm = pe.transpose(ps[:, 7, tok(b)], index_raw[:, tok(b)], ident)
            mm.then_inc(index_turned, 1)
            pe.wait_ge(index_ready, 1)
            item = 0
            for b in range(1, NB):
                for hd in range(HEADS):
                    if item >= 4:
                        pe.wait_ge(relu_done, n.next(relu_done))
                    r = slice(64 * (hd % 2), 64 * (hd % 2) + 64)
                    pe.matmul(ps[:, 4 + item % 4, 0:(b + 1) * P], q_chunk(E_QI + hd // 2)[r, tok(b)],
                              q_chunk(E_KI)[r, 0:(b + 1) * P], start=True, stop=True).then_inc(scores_ready, 1)
                    item += 1
            n.next(relu_done, 4)
            stage_gemm("e_qk", wait=False)
            values("e_v")
            stage_gemm("e_conv", wait=False)
            stage_gemm("e_gate", wait=False)
            pe.wait_ge(relu_done, n.seen["relu_done"])
            pe.wait_ge(tables_landed, 16)
            pe.wait_ge(even_ready, 1)
            attention("dsa")
            stage_gemm("e_out", order=(4, 5, 6, 7, 0, 1, 2, 3))
            ln_stat()
            for part in "ab":
                stage_gemm(f"up2{part}", wait=part == "a")
                stage_down(f"down2{part}")
            ln_stat()
            t0 = stages["o_in"][2]
            w = slot_of("o_in", Step(0))
            banks = [open_tile(t0, Step(0), 2, i) for i in range(2)]
            for k in range(DC):
                pe.wait_ge(x_ready, n.next(x_ready))
                for i in range(2):
                    mm = product(banks[i], plain_cols(w, i, k), xu(k), k == 0, k == DC - 1)
                    if k == DC - 1:
                        mm.then_inc(tile_done, 1)
            for j in range(1, 5):
                w = slot_of("o_in", Step(j))
                width = 256 if j < 4 else 160
                for i in range(2):
                    bank = open_tile(t0, Step(j), 2, i)
                    at = 32 if (j, i) == (4, 1) else i * P
                    for k in range(DC):
                        mm = product(bank, halves(w, lambda t: t[:, k * width + at:k * width + at + P]), xu(k), k == 0, k == DC - 1)
                    mm.then_inc(tile_done, 1)
            for i in range(5):
                pe.wait_ge(squared, n.next(squared))
                mm = pe.matmul(ps[:, 4 if i < 3 else 5], ones, sq[i % 2], start=i in (0, 3), stop=i in (2, 4))
                mm.then_inc(stat_done, 1)
            pe.wait_ge(rope_raw, 1)
            pe.matmul(ps[0:QK_DIM, 6], key_rot, k_rope_raw, start=True, stop=True)
            pe.matmul(ps[0:QK_DIM, 7], key_move, k_rope_raw, start=True, stop=True).then_inc(rope_mm, 1)
            t0 = stages["o_uq"][2]
            pe.wait_ge(lat_ready, 3)
            for j in range(5):
                if j < 4:
                    w = raw_slot("o_uq", j)
                    for i in range(2):
                        bank = open_tile(t0, Step(j), 2, i)
                        for k in range(3):
                            mm = pe.matmul(bank[0:QK_DIM], w[:, k * 192 + i * QK_DIM:k * 192 + (i + 1) * QK_DIM], lat[k], start=k == 0, stop=k == 2)
                        mm.then_inc(tile_done, 1)
                if j >= 1:
                    for hd in (2 * j - 2, 2 * j - 1):
                        pe.wait_ge(rope_raw, hd + 2)
                        pe.wait_ge(rope_used, max(hd, 1))
                        pe.matmul(ps[0:QK_DIM, 6 + (hd + 1) % 2], rot[0:QK_DIM], act[0:QK_DIM, hd * S:(hd + 1) * S], start=True, stop=True).then_inc(rope_mm, 1)
            pe.wait_ge(pool_ready, 4)
            w = raw_slot("o_pool")
            t0 = stages["o_pool"][2]
            for g in range(4):
                bank = open_tile(t0, Step(0), 4, g)
                pe.matmul(bank, w[:, g * P:(g + 1) * P], pool_in[g][:, 16:], start=True, stop=True).then_inc(tile_done, 1)
            pe.wait_ge(lat_ready, 5)
            w = raw_slot("o_ukv")
            t0 = stages["o_ukv"][2]
            wk = w[:].rearrange("p (c h n) -> p c h n", c=2, h=HEADS)
            for hd in range(HEADS):
                bank = open_tile(t0, Step(0), 12, hd)
                for k in range(2):
                    mm = pe.matmul(bank[0:NOPE], wk[:, k, hd, 0:NOPE], lat[3 + k], start=k == 0, stop=k == 1)
                mm.then_inc(tile_done, 1)
            for b in range(NB):
                bank = open_tile(t0, Step(0), 12, HEADS + b)
                for k in range(2):
                    mm = pe.matmul(bank.rearrange("p (h n) -> p h n", h=HEADS), lat[3 + k][:, tok(b)], wk[:, k, :, NOPE:P], start=k == 0, stop=k == 1)
                mm.then_inc(tile_done, 1)
            pe.wait_ge(odd_ready, 1)
            attention("mla")
            stage_gemm("o_out")
            ln_stat()
            for part in "ab":
                stage_gemm(f"up3{part}", wait=part == "a")
                stage_down(f"down3{part}")
            ln_stat()

        @block.vector
        def _(dve):
            n = Tally()
            link = Chain(dve, d_chain)
            items = [0]

            def read_tile(st, f):
                dve.wait_ge(tile_done, st.at(lambda j: f(j) + 1))
                return ps[:, f(st.first) % BANKS]

            def one_tile(t):
                return read_tile(Step(0), lambda _: t)

            def sums_begin(ln):
                dve.memset(sum2, 0.0).then_inc(summed, 1)
                if ln:
                    dve.memset(sum1, 0.0).then_inc(summed, 1)
                return n.take(summed, 18 if ln else 9), n.take(squared, DC)

            def sums_add(st, base, src, ln):
                s0, q0 = base
                if ln:
                    dve.wait_ge(summed, st.at(lambda j: s0 + 2 + 2 * j))
                    dve.tensor_tensor(sum1, sum1, src, ALU.add).then_inc(summed, 1)
                dve.wait_ge(squared, st.at(lambda j: q0 + j + 1))
                if not ln:
                    dve.wait_ge(summed, st.at(lambda j: s0 + 1 + j))
                dve.tensor_tensor(sum2, sum2, sq[st.first % 2], ALU.add).then_inc(summed, 1)

            def low(t, hi, lo, count):
                dve.wait_ge(hi_done, count)
                dve.tensor_tensor(lo, t, hi.bitcast(F32), ALU.subtract).then_inc(x_ready, 1)

            def low_u(c, count, t=None):
                low(sq[c % 2] if t is None else t, chunk(u_hi, c), chunk(u_lo, c), count)

            def rms_apply(gain, gain_at):
                i0, x0 = n.take(hi_done, DC), n.take(x_ready, DC)
                n.take(t_ready, DC)
                dve.wait_ge(rinv_done, n.next(rinv_done))
                for c in range(DC + 1):
                    if c < DC:
                        if c >= 2 or x0:
                            dve.wait_ge(x_ready, x0 + max(c - 1, 0))
                        dve.scalar_tensor_tensor(sq[c % 2], chunk(h, c), pcol(gain, gain_at + c), rinv[0],
                                                 ALU.mult, ALU.mult).then_inc(t_ready, 1)
                    if c >= 1:
                        low_u(c - 1, i0 + c)

            def ln_apply(src, gain, gain_at, last=False):
                mean, var = sum1, sum2
                i0 = n.take(hi_done, 0 if last else DC)
                n.take(x_ready, 0 if last else DC)
                dve.wait_ge(mean_done, n.next(mean_done))
                link(dve.tensor_tensor(rinv[1], mean, mean, ALU.mult))
                link(dve.scalar_tensor_tensor(var, ps[:, 5], 1.0 / D, rinv[1], ALU.mult, ALU.subtract))
                link(dve.tensor_scalar(var, var, 0.0, None, ALU.max))
                dve.sem_inc(var_done, 1)
                dve.wait_ge(rinv_done, n.next(rinv_done))
                for c in range(DC + 1):
                    if c < DC:
                        t = act_tmp[c % 2]
                        if c >= 2:
                            if last:
                                dve.wait_ge(h_out, c - 1)
                            else:
                                dve.wait_ge(hi_done, i0 + c - 1)
                        link(dve.tensor_tensor(t, chunk(src, c), mean, ALU.subtract))
                        dve.scalar_tensor_tensor(t, t, pcol(gain, gain_at + c), rinv[0],
                                                 ALU.mult, ALU.mult).then_inc(xn_ready, 1)
                    if c >= 1 and not last:
                        low_u(c - 1, i0 + c)

            def residual(name, bias=None, gate=None, first=True, sums=True):
                t0 = stages[name][2]
                ln = gate is not None
                base = sums_begin(ln) if sums else None
                link.begin(1 if ln and first else 0)

                def body(st):
                    link.step(st)
                    bank = read_tile(st, lambda j: t0 + j)
                    hc = chunk_at(h, st, lambda j: j)
                    if ln:
                        g = mod[:, gate + st.first:gate + st.first + 1] if st.counter is None else \
                            mod[:, bass.ds(st.at(lambda j: gate + j), 1)]
                        if first:
                            t = act_tmp[st.first % 2]
                            link(dve.tensor_scalar(t, bank, g, None, ALU.mult))
                            dve.scalar_tensor_tensor(hc, hc, DN_ALPHA, t, ALU.mult, ALU.add).then_inc(tile_used, 1)
                        else:
                            dve.scalar_tensor_tensor(hc, bank, g, hc, ALU.mult, ALU.add).then_inc(tile_used, 1)
                        if sums:
                            dve.wait_ge(tile_used, st.at(lambda j: BANKS + t0 + j + 1))
                    elif bias is not None:
                        dve.scalar_tensor_tensor(hc, bank, pcol_at(bias, st, lambda j: j), hc,
                                                 ALU.add, ALU.add).then_inc(tile_used, 1)
                    else:
                        dve.tensor_tensor(hc, bank, hc, ALU.add).then_inc(tile_used, 1)
                    if sums:
                        sums_add(st, base, hc, ln)

                run_steps(dve, DC, body, 4)
                link.end(DC)

            def ada_step(layer, st, jj):
                first = jj(st.first)
                s = first % 4
                if st.counter is None:
                    acc = arena[:, first // 4 * D:(first // 4 + 1) * D]
                else:
                    acc = arena[:, bass.ds(st.at(lambda j: (jj(j) - s) // 4 * D), D)]
                for kk in range(2):
                    dve.wait_ge(ada_landed[kk], st.at(lambda j: 16 * (layer * 24 + jj(j) + 1)))
                    by = cond[:, 2 * s + kk:2 * s + kk + 1]
                    if s == 0 and kk == 0:
                        link(dve.tensor_scalar(acc, ada_slot[kk], by, None, ALU.mult))
                    else:
                        link(dve.scalar_tensor_tensor(acc, ada_slot[kk], by, acc, ALU.mult, ALU.add))
                    dve.sem_inc(ada_used, 1)

            def up_stage(i, part):
                t0 = stages[f"up{i}{part}"][2]
                a0, y0, i0, x0 = [n.take(s_, HC) for s_ in (act_done, t_ready, hi_done, x_ready)]
                jj = (lambda j: j) if part == "a" else (lambda j: j + HC)
                dve.wait_ge(cond_ready, 1)

                def body(st):
                    link.step(st)
                    bank = read_tile(st, lambda j: t0 + 2 * j + 1)
                    dve.wait_ge(act_done, st.at(lambda j: a0 + j + 1))
                    t = sq[st.first % 2]
                    dve.wait_ge(x_ready, st.at(lambda j: x0 + j))
                    dve.tensor_tensor(t, act_tmp[st.first % 2], bank, ALU.mult).then_inc(t_ready, 1)
                    dve.wait_ge(t_ready, st.at(lambda j: y0 + j + 1))
                    dve.sem_inc(tile_used, 2)
                    low(t, chunk_at(act_hi, st, lambda j: j), chunk_at(act_lo, st, lambda j: j), st.at(lambda j: i0 + j + 1))
                    ada_step(i, st, jj)

                link.begin(2)
                run_steps(dve, HC, body, 4)
                link.end(HC)
                if part == "b":
                    link.begin(0)
                    for j in (HC, HC + 1):
                        ada_step(i, Step(j), jj)
                    dve.sem_inc(ada_summed, 1)

            def up_conv_stage(i, layer, part):
                t0 = stages[f"up{i}{part}"][2]
                a0, i0, x0 = n.take(act_done, 3 * HC), n.take(hi_done, HC), n.take(x_ready, HC)
                n.take(t_ready, HC)
                z = 0 if part == "a" else HC

                def body(st):
                    link.step(st)
                    par_ = st.first % 2
                    tiles = [(act_tmp[par_], z), (rinv[par_], FC + z)]
                    banks = [read_tile(st, lambda j: t0 + 2 * j), read_tile(st, lambda j: t0 + 2 * j + 1)]
                    dve.wait_ge(act_done, st.at(lambda j: a0 + 3 * j + 2))
                    for back in (1, 2):
                        for (y, at), bank in zip(tiles, banks):
                            spare = 0 if back == 2 and y is tiles[1][0] else 1
                            tap = pcol_at("ffn_conv_w", st, lambda j: layer * 132 + (at + j) * 3 + 2 - back)
                            link(dve.scalar_tensor_tensor(y[:, back:], bank[:, 0:S - back], tap, y[:, back:], ALU.mult, ALU.add), spare)
                    dve.sem_inc(h_ready, 1)
                    dve.sem_inc(tile_used, 2)
                    dve.wait_ge(act_done, st.at(lambda j: a0 + 3 * j + 3))
                    dve.wait_ge(x_ready, st.at(lambda j: x0 + j))
                    dve.tensor_tensor(sq[par_], act_tmp[par_], rinv[par_], ALU.mult).then_inc(t_ready, 1)
                    low(sq[par_], chunk_at(act_hi, st, lambda j: j), chunk_at(act_lo, st, lambda j: j), st.at(lambda j: i0 + j + 1))

                link.begin(4)
                run_steps(dve, HC, body, 4)
                link.end(HC)

            def ple_stage(i, sums):
                t0 = stages[f"ple{i}"][2]
                a0 = n.take(act_done, DC)
                if sums:
                    base = sums_begin(False)
                link.begin(1)

                def body(st):
                    link.step(st)
                    bank = read_tile(st, lambda j: t0 + 2 * j + 1)
                    dve.wait_ge(act_done, st.at(lambda j: a0 + j + 1))
                    t = act_tmp[st.first % 2]
                    link(dve.tensor_tensor(t, t, bank, ALU.mult))
                    hc = chunk_at(h, st, lambda j: j)
                    dve.tensor_tensor(hc, hc, t, ALU.add).then_inc(tile_used, 2)
                    if sums:
                        sums_add(st, base, hc, False)

                run_steps(dve, DC, body, 4)
                link.end(DC)

            def mod_stage(layer):
                link.begin(0)
                dve.wait_ge(mod_done, n.next(mod_done))
                m = mod[:, layer * 48:(layer + 1) * 48]
                at = PARAM_AT["ada_b"] + layer * 48
                link(dve.tensor_tensor(m, ps[:, 6, 0:48], par[:, at:at + 48], ALU.add))
                link(dve.tensor_scalar(m[:, 8:24], m[:, 8:24], 1.0, None, ALU.add))
                link(dve.tensor_scalar(m[:, 32:48], m[:, 32:48], 1.0, None, ALU.add))
                dve.sem_inc(mod_ready, 1)

            def attention(kind):
                link.begin(0)
                G, C, norm = ATT[kind]["heads"], ATT[kind]["comps"], ATT[kind]["norm"]
                e0, t0 = n.take(exp_done, 4 * C * G), n.take(turned, 4 * G)
                o0, s0 = n.take(o_done, G), n.take(scaled, 4 * G)
                n.take(squared, G if norm else 0)
                i0, x0 = [n.take(s_, G if norm else G // 2) for s_ in (hi_done, x_ready)]
                n.take(t_ready, G if norm else 0)
                out0 = 4 if kind == "mla" else 0

                def reciprocals(g):
                    dve.wait_ge(exp_done, e0 + (g + 1) * 4 * C)
                    if g > 0:
                        dve.wait_ge(scaled, s0 + 4 * g)
                    if C == 2:
                        if g > 0:
                            dve.wait_ge(mixed, 4 * g)
                        link(dve.reciprocal(rowinv[:, 4:8], rowsum[:, 4:8]))
                        link(dve.tensor_scalar(rowinv[:, 4:8], rowinv[:, 4:8], lam[:, 6:7], None, ALU.mult))
                    dve.reciprocal(rowinv[:, 0:4], rowsum[:, 0:4]).then_inc(inv_done, 1)

                def mix(g):
                    for b in range(NB):
                        dve.wait_ge(scaled, s0 + 4 * g + b + 1)
                        dve.scalar_tensor_tensor(probs(kind, g, 0, b), probs(kind, g, 1, b), rowinv[:, 4 + b:5 + b],
                                                 probs(kind, g, 0, b), ALU.mult, ALU.add).then_inc(mixed, 1)

                for g in range(G + 4 if norm else G + 3):
                    if C == 2 and g == G:
                        mix(G - 1)
                    if g < G:
                        for i in range(4 * C):
                            b = i % 4
                            if i == 4 and g > 0:
                                mix(g - 1)
                            dve.wait_ge(scores_ready, n.next(scores_ready))
                            if g > 0:
                                dve.wait_ge(exp_done, e0 + (g - 1) * 4 * C + i + 1)
                            dve.tensor_reduce(nmax[:, i:i + 1], ps[:, 4 + items[0] % 4, 0:(b + 1) * P],
                                              AX.X, ALU.max, negate=True).then_inc(max_done, 1)
                            items[0] += 1
                    if g < G and C == 2:
                        reciprocals(g)
                    for kc in (0, 3):
                        if 0 <= g - 1 < G:
                            dve.wait_ge(turned, t0 + 4 * (g - 1) + kc + 1)
                            if g - 1 >= 2:
                                dve.wait_ge(o_done, o0 + g - 2)
                            dve.tensor_copy(probs_t(kind, g - 1, kc), ps[:, kc % 2, 0:(NB - kc) * P]).then_inc(turned_dve, 1)
                        if kc == 0 and g < G and C == 1:
                            reciprocals(g)
                    if norm and 0 <= g - 4 < G:
                        low_u(g - 4, i0 + g - 3, act_tmp[g % 2])
                    if not norm and g % 2 == 0 and g >= 4:
                        low_u(out0 + g // 2 - 2, i0 + g // 2 - 1, act_tmp[g // 2 % 2])
                    if 0 <= g - 2 < G:
                        dve.wait_ge(o_done, o0 + g - 1)
                        if kind == "diff":
                            if g >= 4:
                                dve.wait_ge(x_ready, x0 + g - 3)
                            dve.tensor_copy(act_tmp[g % 2], ps[:, 2]).then_inc(o_copied, 1)
                        elif g % 2 == 1:
                            if g >= 7:
                                dve.wait_ge(x_ready, x0 + (g - 3) // 2 - 1)
                            dve.tensor_copy(act_tmp[(g - 3) // 2 % 2], ps[:, 2]).then_inc(o_copied, 1)
                    if norm and 0 <= g - 3 < G:
                        dve.wait_ge(rinv_done, n.next(rinv_done))
                        o = act_tmp[(g - 3) % 2]
                        dve.scalar_tensor_tensor(o, o, lam[:, 7:8], rinv[(g - 3) % 2], ALU.mult, ALU.mult).then_inc(t_ready, 1)

            dve.wait_ge(inputs_landed, 64)
            dve.memset(v_sb[BUCKETS:BUCKETS + 1, 0:HEADS], NEG).then_inc(bias_in, 1)
            lq = PARAM_AT["lambda"]
            link(dve.tensor_scalar(pcol("q_norm_g"), pcol("q_norm_g"), 64 ** -0.5, None, ALU.mult))
            link(dve.tensor_tensor(lam[:, 0:1], par[:, lq:lq + 1], par[:, lq + 1:lq + 2], ALU.mult))
            dve.tensor_tensor(lam[:, 1:2], par[:, lq + 2:lq + 3], par[:, lq + 3:lq + 4], ALU.mult).then_inc(lam_in, 1)
            dve.wait_ge(bias_mm, 1)
            link(dve.tensor_copy(act[0:HEADS, 20 * S:21 * S], ps[0:HEADS, 6]))
            dve.tensor_copy(act[0:HEADS, 21 * S:21 * S + P], ps[0:HEADS, 7, 0:P]).then_inc(bias_sb, 1)
            dve.wait_ge(lam_exp, 1)
            link(dve.tensor_tensor(lam[:, 4:5], lam[:, 3:4], lam[:, 2:3], ALU.subtract))
            link(dve.tensor_scalar(lam[:, 6:7], lam[:, 4:5], LAMBDA_INIT, None, ALU.subtract))
            link(dve.tensor_scalar(lam[:, 7:8], pcol("sub_norm_g"), 1.0 - LAMBDA_INIT, None, ALU.mult))
            base = sums_begin(False)
            for c in range(DC):
                sums_add(Step(c), base, chunk(h, c), False)
            rms_apply("conv_norm_g", 0)
            for i in range(2):
                link(dve.memset(conv_in[i][:, 0:CONV - 1], 0.0))
            t0 = stages["pw1"][2]
            a0 = n.take(act_done, DC)
            base = sums_begin(True)
            link.begin(CONV - SIDE + 3)

            def conv_step(st):
                link.step(st)
                bank = read_tile(st, lambda j: t0 + 2 * j)
                cin = conv_in[st.first % 2]
                dve.wait_ge(act_done, st.at(lambda j: a0 + j + 1))
                link(dve.scalar_tensor_tensor(cin[:, CONV - 1:], bank, pcol_at("conv_b_pw1", st, lambda j: j),
                                              act_tmp[st.first % 2], ALU.add, ALU.mult))
                dve.sem_inc(tile_used, 2)
                dve.sem_inc(conv_in_ready, 1)
                y = chunk_at(conv_out, st, lambda j: j)
                for t in range(CONV - SIDE):
                    tap = pcol_at("conv_dw_w", st, lambda j: j * CONV + t)
                    if t == 0:
                        link(dve.tensor_scalar(y, cin[:, 0:S], tap, pcol_at("conv_dw_b", st, lambda j: j), ALU.mult, ALU.add), 1)
                    elif t == 1:
                        link(dve.tensor_scalar(conv_odd, cin[:, t:t + S], tap, None, ALU.mult), 1)
                    else:
                        acc = (y, conv_odd)[t % 2]
                        link(dve.scalar_tensor_tensor(acc, cin[:, t:t + S], tap, acc, ALU.mult, ALU.add), 1 if t < CONV - SIDE - 1 else 0)
                link(dve.tensor_tensor(y, y, conv_odd, ALU.add))
                dve.wait_ge(side_added, st.at(lambda j: (j + 1) * (SIDE - 1)))
                link(dve.tensor_tensor(y, y, side_acc[st.first % 2], ALU.add))
                dve.sem_inc(side_used, 1)
                dve.sem_inc(h_ready, 1)
                sums_add(st, base, y, True)

            run_steps(dve, DC, conv_step, 4)
            link.end(DC)
            link.begin(0)
            ln_apply(conv_out, "conv_ln_g", 0)
            residual("pw2", bias="conv_b_pw2")
            for i in range(2):
                rms_apply("ffn_norm_g", i * DC)
                if i == 0:
                    dve.wait_ge(bias_stored, 16)
                for part in "ab":
                    up_stage(i, part)
                    residual(f"down{i}{part}", sums=part == "b")
                dve.wait_ge(p_rounded, i + 1)
                dve.tensor_tensor(p_lo[:], p_sb[:, 0:2 * S], p_hi[:].bitcast(F32), ALU.subtract).then_inc(p_ready, 1)
                rms_apply("ple_norm_g", i * DC)
                ple_stage(i, sums=i == 0)
                if i == 1:
                    break
                rms_apply("attn_norm_g", 0)
                mod_stage(0)
                n.take(squared, 2 * DC)
                t0 = stages["qk"][2]
                for j in range(9):
                    if j < 8:
                        for t in (2 * j, 2 * j + 1):
                            dve.tensor_copy(chunk(act, t), one_tile(t0 + t)).then_inc(tile_used, 1)
                    if j >= 1:
                        for t in (2 * j - 2, 2 * j - 1):
                            dve.wait_ge(rinv_done, n.next(rinv_done))
                            dve.scalar_tensor_tensor(chunk(act, t), chunk(act, t), pcol("q_norm_g" if t < 8 else "k_norm_g"),
                                                     rinv[t % 2], ALU.mult, ALU.mult).then_inc(qk_normed, 1)
                t0 = stages["v"][2]
                vv = v_sb[:].rearrange("p (b n) -> p b n", b=NB)
                for t in range(8):
                    dve.tensor_copy(vv[:, 2 * (t % 2):2 * (t % 2) + 2, t // 2 * 256:(t // 2 + 1) * 256],
                                    one_tile(t0 + t).rearrange("p (b n) -> p b n", b=2)).then_inc(tile_used, 1)
                attention("diff")
                residual("wo")

            link.begin(0)
            i0, _ = n.take(hi_done, DC), n.take(x_ready, DC)
            for c in range(DC):
                low_u(c, i0 + c + 1)
            mod_stage(1)
            t0 = stages["e_index"][2]
            for t in range(5):
                link(dve.tensor_copy(chunk(act, E_QI + t), one_tile(t0 + t)))
                dve.sem_inc(tile_used, 1)
            link(dve.tensor_copy(index_raw, one_tile(t0 + 5)))
            dve.sem_inc(tile_used, 1)
            dve.sem_inc(index_copied, 1)
            dve.wait_ge(index_turned, 1)
            link(dve.tensor_scalar(index_w.rearrange("p (b n) -> p b n", b=NB), ps[:, 7].rearrange("p (b n) -> p b n", b=NB)[:, :, P - 8:P],
                                   (HEADS * 64) ** -0.5, None, ALU.mult))
            dve.sem_inc(index_ready, 1)
            scores = [None] + [chunk(act, E_SC + b - 1) for b in range(1, NB)]
            for b in range(1, NB):
                nk = (b + 1) * P
                sc = scores[b][:, 0:nk]
                for hd in range(HEADS):
                    i = (b - 1) * HEADS + hd
                    dve.wait_ge(relu_done, n.next(relu_done))
                    w_col = index_w[:, b * 8 + hd:b * 8 + hd + 1]
                    if hd == 0:
                        link(dve.tensor_scalar(sc, act_tmp[i % 2][:, 0:nk], w_col, None, ALU.mult))
                    else:
                        link(dve.scalar_tensor_tensor(sc, act_tmp[i % 2][:, 0:nk], w_col, sc, ALU.mult, ALU.add))
                    dve.sem_inc(relu_used, 1)
                link(dve.tensor_tensor(sc[:, nk - P:nk], sc[:, nk - P:nk], chunkmask, ALU.add))
            n.take(scores_ready, 3 * HEADS)
            link(dve.tensor_copy(masks[:, 0:P], chunkmask))
            best = small[:, 32:40]
            rounds = [(b, r) for b in range(1, NB) for r in range(TOPK // 8)]

            def topk_rounds(count):
                for _ in range(min(count, len(rounds))):
                    b, r = rounds.pop(0)
                    nk = (b + 1) * P
                    sc = scores[b][:, 0:nk]
                    link(dve.max(best, sc))
                    link(dve.match_replace(sc, best, sc, TAKEN))
                    if r == TOPK // 8 - 1:
                        m = masks[:, b * S:b * S + nk]
                        link(dve.tensor_scalar(m, sc, TAKEN, 1.0, ALU.is_equal, ALU.subtract))
                        link(dve.tensor_scalar(m, m, -NEG, None, ALU.mult))
                        link(dve.tensor_tensor(m[:, nk - P:nk], m[:, nk - P:nk], chunkmask, ALU.add))

            t0 = stages["e_qk"][2]
            for t in range(8):
                if t < 4:
                    link(dve.tensor_scalar(chunk(act, E_Q + t), one_tile(t0 + t), 64 ** -0.5, None, ALU.mult))
                else:
                    link(dve.tensor_copy(chunk(act, E_K + t - 4), one_tile(t0 + t)))
                dve.sem_inc(tile_used, 1)
                topk_rounds(2)
            t0 = stages["e_v"][2]
            vv = v_sb[:, 0:NB * S].rearrange("p (b n) -> p b n", b=NB)
            for t in range(4):
                link(dve.tensor_copy(vv[:, 2 * (t % 2):2 * (t % 2) + 2, t // 2 * 256:(t // 2 + 1) * 256],
                                     one_tile(t0 + t).rearrange("p (b n) -> p b n", b=2)))
                dve.sem_inc(tile_used, 1)
                topk_rounds(2)
            t0 = stages["e_conv"][2]
            link(dve.memset(e_pad[:, 0:2], 0.0))
            a0 = n.take(act_done, 4)
            for j in range(4):
                bank = one_tile(t0 + 2 * j + 1)
                dve.wait_ge(act_done, a0 + j + 1)
                link(dve.tensor_tensor(e_pad[:, 2:], act_tmp[j % 2], bank, ALU.mult))
                dve.sem_inc(tile_used, 2)
                y = chunk(act, E_CV + j)
                link(dve.tensor_scalar(y, e_pad[:, 0:S], pcol("ev_conv_w", j * 3), None, ALU.mult))
                for t in (1, 2):
                    link(dve.scalar_tensor_tensor(y, e_pad[:, t:t + S], pcol("ev_conv_w", j * 3 + t), y, ALU.mult, ALU.add))
                topk_rounds(4)
            t0 = stages["e_gate"][2]
            for t in range(4):
                y = chunk(act, E_CV + t)
                link(dve.tensor_tensor(y, one_tile(t0 + t), y, ALU.mult))
                dve.sem_inc(tile_used, 1)
                dve.sem_inc(t_ready, 1)
                topk_rounds(4)
            topk_rounds(len(rounds))
            i0, _ = n.take(hi_done, 4), n.take(x_ready, 4)
            n.take(t_ready, 4)
            for t in range(4):
                low_u(4 + t, i0 + t + 1, chunk(act, E_CV + t))
            dve.sem_inc(even_ready, 1)
            attention("dsa")
            residual("e_out", gate=16)
            ln_apply(h, "ln_mix_g", 0)
            for part in "ab":
                up_conv_stage(2, 0, part)
                residual(f"down2{part}", gate=40, first=part == "a", sums=part == "b")
            ln_apply(h, "ln_ffn_g", 0)

            link.begin(0)
            n.take(squared, 5)
            t0 = stages["o_in"][2]
            for g in range(4):
                link(dve.memset(pool_in[g][:, 0:16], 0.0))
                link(dve.tensor_copy(pool_in[g][:, 16:], one_tile(t0 + g)))
                dve.sem_inc(tile_used, 1)
            for i in range(5):
                link(dve.tensor_copy(lat[i], one_tile(t0 + 4 + i)))
                dve.sem_inc(tile_used, 1)
            link(dve.tensor_copy(k_rope_raw, one_tile(t0 + 9)))
            dve.sem_inc(tile_used, 1)
            dve.sem_inc(rope_raw, 1)
            for i in range(5):
                if i in (0, 3):
                    dve.wait_ge(rinv_done, n.next(rinv_done))
                dve.scalar_tensor_tensor(lat[i], lat[i], pcol("lat_g", i), rinv[0 if i < 3 else 1],
                                         ALU.mult, ALU.mult).then_inc(lat_ready, 1)
            sums_of = [tmp[:, 2 * S:2 * S + POOLW], tmp[:, 6 * S:6 * S + POOLW]]
            first = small[:, 0:16]
            for g, win in enumerate(WINDOWS):
                src, k = pool_in[g], 1
                while k < win:
                    dst = sums_of[(k.bit_length() - 1) % 2]
                    lo = 2 * k - 1
                    link(dve.tensor_tensor(dst[:, lo:], src[:, lo:], src[:, lo - k:POOLW - k], ALU.add))
                    src, k = dst, 2 * k
                x = pool_in[g][:, 16:]
                at = CONST_AT["first_counts"] + g * 16
                link(dve.tensor_tensor(first, src[:, 16:32], con[:, at:at + 16], ALU.mult))
                link(dve.tensor_tensor(first, first, x[:, 0:16], ALU.subtract))
                link(dve.scalar_tensor_tensor(x, src[:, 16:], 1.0 / win, x, ALU.mult, ALU.subtract))
                link(dve.tensor_copy(x[:, 0:16], first))
                dve.sem_inc(pool_ready, 1)
            rows = slice(NOPE, QK_DIM)
            cos, sin = rope_tab[rows, 0:S], rope_tab[rows, S:2 * S]
            turned_part, moved_part = act_tmp[0][rows], act_tmp[1][rows]
            dve.wait_ge(tables_landed, 32)
            dve.wait_ge(rope_mm, 1)
            link(dve.tensor_tensor(turned_part, ps[rows, 6], sin, ALU.mult))
            link(dve.tensor_tensor(moved_part, ps[rows, 7], cos, ALU.mult))
            dve.sem_inc(rope_used, 1)
            link(dve.tensor_tensor(moved_part, moved_part, turned_part, ALU.add))
            for g in range(HEADS):
                link(dve.tensor_copy(act[rows, (8 + g) * S:(9 + g) * S], moved_part))
            t0 = stages["o_uq"][2]
            for j in range(5):
                if j < 4:
                    for hd in (2 * j, 2 * j + 1):
                        link(dve.tensor_scalar(act[0:QK_DIM, hd * S:(hd + 1) * S], one_tile(t0 + hd)[0:QK_DIM], QK_DIM ** -0.5, None, ALU.mult))
                        dve.sem_inc(tile_used, 1)
                        dve.sem_inc(rope_raw, 1)
                if j >= 1:
                    for hd in (2 * j - 2, 2 * j - 1):
                        q = act[rows, hd * S:(hd + 1) * S]
                        dve.wait_ge(rope_mm, hd + 2)
                        link(dve.tensor_tensor(turned_part, ps[rows, 6 + (hd + 1) % 2], sin, ALU.mult))
                        dve.sem_inc(rope_used, 1)
                        link(dve.tensor_tensor(q, q, cos, ALU.mult))
                        link(dve.tensor_tensor(q, q, turned_part, ALU.add))
            t0 = stages["o_pool"][2]
            i0, x0 = n.take(hi_done, 4), n.take(x_ready, 4)
            n.take(t_ready, 4)
            for g in range(5):
                if g < 4:
                    dve.wait_ge(x_ready, x0 + max(g - 1, 0))
                    dve.tensor_scalar(sq[g % 2], one_tile(t0 + g), pcol("pool_scale", g), None, ALU.mult).then_inc(t_ready, 1)
                if g >= 1:
                    low_u(g - 1, i0 + g)
                    dve.sem_inc(tile_used, 1)
            t0 = stages["o_ukv"][2]
            for hd in range(HEADS):
                link(dve.tensor_copy(act[0:NOPE, (8 + hd) * S:(9 + hd) * S], one_tile(t0 + hd)[0:NOPE]))
                dve.sem_inc(tile_used, 1)
            for b in range(NB):
                link(dve.tensor_copy(chunk(v_sb, b), one_tile(t0 + HEADS + b)))
                dve.sem_inc(tile_used, 1)
            dve.sem_inc(odd_ready, 1)
            attention("mla")
            residual("o_out", gate=48 + 16)
            ln_apply(h, "ln_mix_g", DC)
            for part in "ab":
                up_conv_stage(3, 1, part)
                residual(f"down3{part}", gate=48 + 40, first=part == "a", sums=part == "b")
            ln_apply(h, "ln_ffn_g", DC, last=True)

        @block.gpsimd
        def _(pool):
            inverses = [0]

            def low_halves(name, first, last):
                k0 = stages[name][0]

                def body(st):
                    j = first + st.first
                    at = lambda x: k0 + first + x
                    r, width = (k0 + j) % RING, slot_width[k0 + j]
                    pool.wait_ge(w_rounded, st.at(lambda x: split_no[at(x)]))
                    pool.tensor_tensor(w_lo[r][:, 0:width], raw[r][:, 0:width], w_hi[(k0 + j) % HI_RING][:, 0:width].bitcast(F32),
                                       ALU.subtract).then_inc(w_ready, 1)

                run_steps(pool, last - first, body, 4, tail=1 if name == "o_in" else 0)

            def normalise(kind):
                for g in range(HEADS):
                    inverses[0] += 1
                    pool.wait_ge(inv_done, inverses[0])
                    for b in range(NB):
                        m = probs(kind, g, 0, b)
                        pool.tensor_scalar(m, m, rowinv[:, b:b + 1], None, ALU.mult).then_inc(scaled, 1)

            def side_sums(c):
                acc = side_acc[c % 2]
                for i in range(1, SIDE):
                    m = c * (SIDE - 1) + i - 1
                    pool.wait_ge(side_ready, c * SIDE + i + 1)
                    if m:
                        pool.wait_ge(side_added, m)
                    pool.tensor_tensor(acc, acc, side_prod[m % 3], ALU.add).then_inc(side_added, 1)

            low_halves("pw1", 0, 2)
            for c in range(DC):
                if c < DC - 2:
                    low_halves("pw1", c + 2, c + 3)
                else:
                    low_halves("pw2", c + 2 - DC, c + 3 - DC)
                side_sums(c)
            low_halves("pw2", 2, 4)
            for name, (_, slots, _) in stages.items():
                if name in UNSPLIT or name in ("pw1", "pw2"):
                    continue
                if name in ("wo", "e_out", "o_out"):
                    low_halves(name, 0, 2)
                    normalise({"wo": "diff", "e_out": "dsa", "o_out": "mla"}[name])
                    low_halves(name, 2, slots)
                else:
                    low_halves(name, 0, slots)

        @block.scalar
        def _(sc):
            n = Tally()
            link = Chain(sc, a_chain)

            def tile_ready(st, f):
                sc.wait_ge(tile_done, st.at(lambda j: f(j) + 1))
                return ps[:, f(st.first) % BANKS]

            def squares(wait, src, ln, loop=True):
                s0 = n.take(summed, 18 if ln else 9)

                def body(st):
                    wait(st)
                    if loop or st.first >= 2:
                        sc.wait_ge(summed, st.at(lambda j: s0 + (2 * j if ln else j)))
                    sc.activation(sq[st.first % 2], chunk_at(src, st, lambda j: j), ACT.Square).then_inc(squared, 1)

                if loop:
                    run_steps(sc, DC, body, 4)
                else:
                    for c in range(DC):
                        body(Step(c))

            def split(k):
                st, f = (Step(0), lambda _: k) if isinstance(k, int) else k
                slot = f(st.first)
                if slot >= n_slots or split_no[slot] == 0:
                    return
                if slot >= HI_RING:
                    sc.wait_ge(tile_done, st.at(lambda j: tiles_after[f(j) - HI_RING]))
                sc.wait_ge(landed[slot % RING], st.at(lambda j: landed_due[f(j)]))
                width = slot_width[slot]
                sc.activation(w_hi[slot % HI_RING][:, 0:width], raw[slot % RING][:, 0:width], ACT.Copy).then_inc(w_rounded, 1)

            def split_after(name, st):
                k0 = stages[name][0]
                split((st, lambda j: k0 + j + HI_RING))

            def high(dst, src):
                sc.activation(dst, src, ACT.Copy).then_inc(hi_done, 1)

            def residual(name, ln, per=2):
                t0 = stages[name][2]

                def wait(st):
                    if st.first >= per and st.first % per == 0:
                        split_after(name, Step(st.first // per - 1))
                    sc.wait_ge(tile_used, BANKS + t0 + st.first + 1)

                squares(wait, h, ln, loop=False)
                split_after(name, Step(DC // per - 1))

            def splits(name):
                for j in range(stages[name][1]):
                    split_after(name, Step(j))

            def inverse_root(src, scale, eps, to, done=rinv_done, mark=None):
                link(sc.activation(to, src, ACT.Ln, bias=eps, scale=scale))
                if mark is not None:
                    sc.sem_inc(mark, 1)
                sc.activation(to, to, ACT.Exp, scale=-0.5).then_inc(done, 1)

            def rms():
                link.begin(0)
                sc.wait_ge(stat_done, n.next(stat_done))
                inverse_root(ps[:, 4], 1.0 / D, eps_rms, rinv[0])
                n.take(x_ready, DC)
                for c in range(DC):
                    sc.wait_ge(t_ready, n.next(t_ready))
                    high(chunk(u_hi, c), sq[c % 2])

            def ln(eps, finish, last=False):
                link.begin(0)
                sc.wait_ge(stat_done, n.next(stat_done, 2))
                sc.activation(sum1, ps[:, 4], ACT.Copy, scale=1.0 / D).then_inc(mean_done, 1)
                sc.wait_ge(var_done, n.next(var_done))
                inverse_root(sum2, 1.0, eps, rinv[0])
                for c in range(DC):
                    sc.wait_ge(xn_ready, n.next(xn_ready))
                    finish(c, act_tmp[c % 2])

            def operand(c, src, func, bias, scale=1.0):
                if c >= 2:
                    sc.wait_ge(x_ready, n.seen.get(x_ready.name, 0) - 1)
                n.next(x_ready)
                sc.activation(sq[c % 2], src, func, bias=bias, scale=scale)
                sc.activation(chunk(u_hi, c), src, func, bias=bias, scale=scale).then_inc(hi_done, 1)

            def to_mixer(c, sh, scl):
                operand(c, chunk(h, c), ACT.Identity, mod[:, sh + c:sh + c + 1], mod[:, scl + c:scl + c + 1])

            def dn_finish(shift_name, at, sh, scl):
                def f(c, xn):
                    hc = chunk(h, c)
                    if sh is None:
                        sc.activation(hc, xn, ACT.Identity, bias=pcol(shift_name, at + c)).then_inc(h_out, 1)
                    else:
                        link(sc.activation(hc, xn, ACT.Identity, bias=pcol(shift_name, at + c)))
                        to_mixer(c, sh, scl)
                return f

            def gates(name, func, which, biased=False):
                t0 = stages[name][2]

                def body(st):
                    bank = tile_ready(st, lambda j: t0 + 2 * j + which)
                    sc.wait_ge(tile_used, st.at(lambda j: BANKS + t0 + 2 * j - 2))
                    bias = pcol_at("conv_b_pw1", st, lambda j: DC + j) if biased else con[:, CONST_AT["zero"]:CONST_AT["zero"] + 1]
                    sc.activation(act_tmp[st.first % 2], bank, func, bias=bias).then_inc(act_done, 1)
                return body

            def ada_load(layer, st, jj):
                first = jj(st.first)
                s_ = first % 4
                for kk in range(2):
                    if first >= 1:
                        sc.wait_ge(ada_used, st.at(lambda j: 2 * (layer * 24 + jj(j) - 1) + kk + 1))
                    at = st.at(lambda j: (jj(j) - s_) // 4 * D)
                    cols = slice(at, at + D) if st.counter is None else bass.ds(at, D)
                    rows = a["ada_w"][layer][(2 * s_ + kk) * P:(2 * s_ + kk + 1) * P]
                    sc.dma_start(ada_slot[kk], rows[:, cols]).then_inc(ada_landed[kk], 16)

            def swiglu(i, part):
                name = f"up{i}{part}"
                y0 = n.take(t_ready, HC)
                n.take(x_ready, HC)
                gate = gates(name, ACT.Silu, 0)
                jj = (lambda j: j + 1) if part == "a" else (lambda j: j + HC + 1)

                def body(st):
                    gate(st)
                    split_after(name, st)
                    sc.wait_ge(t_ready, st.at(lambda j: y0 + j + 1))
                    high(chunk_at(act_hi, st, lambda j: j), sq[st.first % 2])
                    ada_load(i, st, jj)

                run_steps(sc, HC, body, 4, tail=2)
                if part == "b":
                    ada_load(i, Step(HC), jj)

            def conv_taps(i, layer, part):
                name = f"up{i}{part}"
                t0 = stages[name][2]
                y0 = n.take(t_ready, HC)
                n.take(x_ready, HC)
                h0 = n.take(h_ready, HC)
                z = 0 if part == "a" else HC
                sc.wait_ge(tile_used, BANKS + t0)

                def body(st):
                    for k, (y, at) in enumerate([(act_tmp[st.first % 2], z), (rinv[st.first % 2], FC + z)]):
                        bank = tile_ready(st, lambda j: t0 + 2 * j + k)
                        tap = pcol_at("ffn_conv_w", st, lambda j: layer * 132 + (at + j) * 3 + 2)
                        sc.activation(y, bank, ACT.Copy, scale=tap).then_inc(act_done, 1)
                    split_after(name, st)
                    sc.wait_ge(h_ready, st.at(lambda j: h0 + j + 1))
                    y = rinv[st.first % 2]
                    sc.activation(y, y, ACT.Silu).then_inc(act_done, 1)
                    sc.wait_ge(t_ready, st.at(lambda j: y0 + j + 1))
                    high(chunk_at(act_hi, st, lambda j: j), sq[st.first % 2])

                run_steps(sc, HC, body, 4, tail=2)

            def attention(kind):
                link.begin(0)
                G, C, norm = ATT[kind]["heads"], ATT[kind]["comps"], ATT[kind]["norm"]
                t0, o0 = n.take(turned, 4 * G), n.take(o_done, G)
                st0 = n.take(stat_done, G if norm else 0)
                y0 = n.take(t_ready, G if norm else 0)
                n.take(x_ready, G if norm else G // 2)
                out0 = 4 if kind == "mla" else 0
                for g in range(G + 4 if norm else G + 3):
                    if g < G:
                        if inverses[0] > 0:
                            sc.wait_ge(inv_done, inverses[0])
                        if g >= 2:
                            sc.wait_ge(turned, t0 + 4 * (g - 1))
                        inverses[0] += 1
                        for i in range(4 * C):
                            comp, b = i // 4, i % 4
                            sc.wait_ge(max_done, n.next(max_done))
                            sc.activation(probs(kind, g, comp, b), ps[:, 4 + items[0] % 4, 0:(b + 1) * P], ACT.Exp,
                                          bias=nmax[:, i:i + 1], accum_out=rowsum[:, i:i + 1]).then_inc(exp_done, 1)
                            items[0] += 1
                    if 0 <= g - 1 < G:
                        for kc in (1, 2):
                            sc.wait_ge(turned, t0 + 4 * (g - 1) + kc + 1)
                            if g - 1 >= 2:
                                sc.wait_ge(o_done, o0 + g - 2)
                            sc.activation(probs_t(kind, g - 1, kc), ps[:, kc % 2, 0:(NB - kc) * P], ACT.Copy).then_inc(turned_act, 1)
                    if norm and 0 <= g - 4 < G:
                        sc.wait_ge(t_ready, y0 + g - 3)
                        high(chunk(u_hi, g - 4), act_tmp[g % 2])
                    if norm and 0 <= g - 2 < G:
                        sc.wait_ge(o_copied, n.next(o_copied))
                        if g - 2 >= 2:
                            sc.wait_ge(stat_done, st0 + g - 3)
                        sc.activation(sq[g % 2], act_tmp[g % 2], ACT.Square).then_inc(squared, 1)
                    if not norm and g % 2 == 1 and g >= 3:
                        sc.wait_ge(o_copied, n.next(o_copied))
                        high(chunk(u_hi, out0 + (g - 3) // 2), act_tmp[(g - 3) // 2 % 2])
                    if norm and 0 <= g - 3 < G:
                        sc.wait_ge(stat_done, st0 + g - 2)
                        if g - 3 >= 2:
                            sc.wait_ge(t_ready, y0 + g - 4)
                        inverse_root(ps[:, 3], 1.0 / P, eps_rms, rinv[(g - 3) % 2], mark=ln_done)

            items, inverses = [0], [0]
            sc.wait_ge(inputs_landed, 64)
            sc.activation(cond, par[:, PARAM_AT["c"]:PARAM_AT["c"] + DC], ACT.Silu).then_inc(cond_ready, 1)
            sc.wait_ge(lam_mm, 1)
            sc.activation(lam[:, 2:4], ps[:, 5, 0:2], ACT.Exp).then_inc(lam_exp, 1)
            sc.wait_ge(x_landed, 16 * DC)
            squares(lambda st: None, h, False, loop=False)
            split(0)
            split(1)
            rms()
            sigmoid = gates("pw1", ACT.Sigmoid, 1, biased=True)
            s0 = n.take(summed, 18)
            for c in range(DC + 1):
                if c < DC:
                    sigmoid(Step(c))
                    split_after("pw1", Step(c))
                if c >= 1:
                    sc.wait_ge(h_ready, n.next(h_ready))
                    sc.wait_ge(summed, s0 + 2 * (c - 1))
                    sc.activation(sq[(c - 1) % 2], chunk(conv_out, c - 1), ACT.Square).then_inc(squared, 1)
                if c < DC:
                    sc.wait_ge(conv_in_ready, c + 1)
                    for i in range(SIDE):
                        t = CONV - SIDE + i
                        m = c * (SIDE - 1) + i - 1
                        if i == 0:
                            to = side_acc[c % 2]
                            if c >= 2:
                                sc.wait_ge(side_used, c - 1)
                        else:
                            to = side_prod[m % 3]
                            if m >= 3:
                                sc.wait_ge(side_added, m - 2)
                        sc.activation(to, conv_in[c % 2][:, t:t + S], ACT.Copy, scale=pcol("conv_dw_w", c * CONV + t)).then_inc(side_ready, 1)
            ln(eps_rms, lambda c, xn: operand(c, xn, ACT.Silu, pcol("conv_ln_b", c)))
            residual("pw2", False)
            for i in range(2):
                rms()
                ada_load(i, Step(0), lambda j: j)
                swiglu(i, "a")
                splits(f"down{i}a")
                swiglu(i, "b")
                residual(f"down{i}b", False, 1)
                sc.wait_ge(p_landed, 16 * (i + 1))
                sc.activation(p_hi[:], p_sb[:, 0:2 * S], ACT.Copy).then_inc(p_rounded, 1)
                rms()
                gate = gates(f"ple{i}", ACT.Sigmoid, 0)
                t0 = stages[f"ple{i}"][2]
                if i == 1:
                    for j in range(DC):
                        gate(Step(j))
                        split_after("ple1", Step(j))
                    break
                s0 = n.take(summed, 9)
                for c in range(DC + 1):
                    if c < DC:
                        gate(Step(c))
                        split_after("ple0", Step(c))
                    if c >= 1:
                        sc.wait_ge(tile_used, BANKS + t0 + 2 * c)
                        sc.wait_ge(summed, s0 + c - 1)
                        sc.activation(sq[(c - 1) % 2], chunk(h, c - 1), ACT.Square).then_inc(squared, 1)
                rms()
                link.begin(0)
                t0 = stages["qk"][2]
                st0 = n.take(stat_done, 16)
                for j in range(9):
                    if j < 8:
                        for t in (2 * j, 2 * j + 1):
                            sc.wait_ge(tile_used, BANKS + t0 + t + 1)
                            if t >= 2:
                                sc.wait_ge(stat_done, st0 + t - 1)
                            sc.activation(sq[t % 2], chunk(act, t), ACT.Square).then_inc(squared, 1)
                        split_after("qk", Step(j))
                    if j >= 1:
                        for t in (2 * j - 2, 2 * j - 1):
                            sc.wait_ge(stat_done, st0 + t + 1)
                            if t >= 2:
                                sc.wait_ge(qk_normed, t - 1)
                            inverse_root(ps[:, 4 + t % 2], 1.0 / 64, eps_rms, rinv[t % 2], mark=ln_done)
                splits("v")
                attention("diff")
                residual("wo", False)
            link.begin(0)
            sc.wait_ge(mod_ready, 1)
            sc.wait_ge(tile_used, BANKS + stages["e_index"][2])
            for c in range(DC):
                to_mixer(c, 0, 8)
            splits("e_index")
            splits("e_keyw")
            for i in range(3 * HEADS):
                nk = (i // HEADS + 2) * P
                sc.wait_ge(scores_ready, 4 * 2 * HEADS + i + 1)
                if i >= 2:
                    sc.wait_ge(relu_used, i - 1)
                sc.activation(act_tmp[i % 2][:, 0:nk], ps[:, 4 + i % 4, 0:nk], ACT.Relu).then_inc(relu_done, 1)
            splits("e_qk")
            splits("e_v")
            sc.wait_ge(relu_used, 3 * HEADS)
            t0 = stages["e_conv"][2]
            for j in range(4):
                bank = tile_ready(Step(0), lambda _: t0 + 2 * j)
                sc.wait_ge(tile_used, BANKS + t0 + 2 * j - 2)
                sc.activation(act_tmp[j % 2], bank, ACT.Copy).then_inc(act_done, 1)
                split_after("e_conv", Step(j))
            splits("e_gate")
            sc.wait_ge(tile_done, stages["e_out"][2])
            n.take(x_ready, 4)
            for t in range(4):
                sc.wait_ge(t_ready, n.next(t_ready))
                high(chunk(u_hi, 4 + t), chunk(act, E_CV + t))
            attention("dsa")
            residual("e_out", True)
            ln(eps_ln, dn_finish("ln_mix_b", 0, 24, 32))
            conv_taps(2, 0, "a")
            splits("down2a")
            conv_taps(2, 0, "b")
            residual("down2b", True, 1)
            ln(eps_ln, dn_finish("ln_ffn_b", 0, 48, 48 + 8))
            link.begin(0)
            splits("o_in")
            t0 = stages["o_in"][2]
            st0 = n.take(stat_done, 5)
            for i in range(5):
                sc.wait_ge(tile_used, BANKS + t0 + 4 + i + 1)
                if i >= 2:
                    sc.wait_ge(stat_done, st0 + i - 1)
                sc.activation(sq[i % 2], lat[i], ACT.Square).then_inc(squared, 1)
                if i == 2:
                    sc.wait_ge(stat_done, st0 + 3)
                    inverse_root(ps[:, 4], 1.0 / QL, eps_rms, rinv[0])
            sc.wait_ge(stat_done, st0 + 5)
            inverse_root(ps[:, 5], 1.0 / KVL, eps_rms, rinv[1])
            n.take(x_ready, 4)
            for g in range(4):
                sc.wait_ge(t_ready, n.next(t_ready))
                high(chunk(u_hi, g), sq[g % 2])
            splits("o_pool")
            splits("o_uq")
            splits("o_ukv")
            attention("mla")
            residual("o_out", True)
            ln(eps_ln, dn_finish("ln_mix_b", DC, 48 + 24, 48 + 32))
            conv_taps(3, 1, "a")
            splits("down3a")
            conv_taps(3, 1, "b")
            residual("down3b", True, 1)
            ln(eps_ln, dn_finish("ln_ffn_b", DC, None, None))


def constant_arrays():
    p = np.arange(P)
    ident = np.eye(P, dtype=np.float32)
    ones64 = (p[:, None] // 64 == p[None, :] // 64).astype(np.float32)
    half = ROPE // 2
    rot = np.zeros((P, QK_DIM), np.float32)
    for i in range(half):
        rot[NOPE + half + i, NOPE + i] = -1.0
        rot[NOPE + i, NOPE + half + i] = 1.0
    key_rot, key_move = np.roll(rot, ROPE, axis=0), np.zeros((P, QK_DIM), np.float32)
    for i in range(ROPE):
        key_move[QK_DIM + i, NOPE + i] = 1.0
    chunkmask = np.where((p[:, None] < 64) & (p[None, :] >= 64), np.float32(NEG), np.float32(0))
    negdist = -np.abs(p[:, None] - np.arange(S)[None, :] + (S - P)).astype(np.float32)
    counts = np.concatenate([1.0 / np.minimum(np.arange(16) + 1, w) for w in WINDOWS]).astype(np.float32)
    cols = [ident, ident[::-1], np.ones((P, P), np.float32), ones64, rot, key_rot, key_move, chunkmask, negdist,
            np.broadcast_to(counts, (P, 64)), np.full((P, 1), EPS_RMS, np.float32), np.full((P, 1), EPS_LN, np.float32),
            np.zeros((P, 1), np.float32)]
    consts = np.ascontiguousarray(np.concatenate(cols, axis=1), dtype=np.float32)
    slopes = np.concatenate([ident * np.float32(2.0 ** (-8.0 * (i + 1) / HEADS)) for i in range(HEADS)], axis=1)
    inv = np.float32(10000.0) ** (-np.arange(0, ROPE, 2, dtype=np.float32) / np.float32(ROPE))
    ang = np.arange(S, dtype=np.float32)[:, None] * inv[None, :]
    table = lambda f: np.tile(np.tile(f(ang).T.astype(np.float32), (2, 1)), (4, 1))
    late = np.ascontiguousarray(np.concatenate([slopes, table(np.cos), table(np.sin)], axis=1), dtype=np.float32)
    dist = S - 1 - np.arange(640)
    nf = np.maximum(dist, 1).astype(np.float32)
    exact = BUCKETS // 2
    large = exact + (np.log(nf / np.float32(exact)) / np.float32(math.log(128 / exact)) * np.float32(BUCKETS - exact)).astype(np.int32)
    bucket = np.where(dist < exact, np.maximum(dist, 0), np.minimum(large, BUCKETS - 1))
    bucket = np.where(dist < 0, BUCKETS, bucket)
    bucket_of = (np.arange(BUCKETS + 1)[:, None] == bucket[None, :]).astype(np.float32)
    return {"consts": consts, "late": late, "bucket_of": bucket_of}


def kernel(**inputs):
    import concourse.bacc as bacc
    from concourse.bass_utils import run_bass_kernel_spmd

    x = {k: np.asarray(v) for k, v in inputs.items()}

    def feature_columns(v):
        return np.reshape(v, (-1, P)).T

    def taps_last(w):
        return np.reshape(w, (w.shape[0], -1, P)).transpose(2, 1, 0).reshape(P, -1)

    def twice(v):
        return np.concatenate([v.reshape(-1), v.reshape(-1)])[:, None]

    lam = np.zeros((P, 4), np.float32)
    for i, name in enumerate(("q1", "k1", "q2", "k2")):
        lam[0:64, i] = x[f"attn_lambda_{name}"][0]
    packed = {
        "conv_norm_g": feature_columns(x["conv_norm_g"]), "conv_b_pw1": feature_columns(x["conv_b_pw1"]),
        "conv_dw_w": taps_last(x["conv_dw_w"][0]), "conv_dw_b": feature_columns(x["conv_dw_b"]),
        "conv_ln_g": feature_columns(x["conv_ln_g"]), "conv_ln_b": feature_columns(x["conv_ln_b"]),
        "conv_b_pw2": feature_columns(x["conv_b_pw2"]), "attn_norm_g": feature_columns(x["attn_norm_g"]),
        "q_norm_g": twice(x["attn_q_norm_g"]), "k_norm_g": twice(x["attn_k_norm_g"]),
        "sub_norm_g": feature_columns(x["attn_sub_norm_g"]), "lambda": lam,
        "ffn_norm_g": feature_columns(x["ffn_norm_g"]), "ple_norm_g": feature_columns(x["ple_norm_g"]),
        "c": feature_columns(x["c_2"]), "ada_b": feature_columns(x["ada_b_2"]),
        "ln_mix_g": feature_columns(x["ln_mix_g_2"]), "ln_mix_b": feature_columns(x["ln_mix_b_2"]),
        "ln_ffn_g": feature_columns(x["ln_ffn_g_2"]), "ln_ffn_b": feature_columns(x["ln_ffn_b_2"]),
        "ev_conv_w": taps_last(x["ev_conv_w_2"][0]), "pool_scale": feature_columns(x["pool_scale_2"]),
        "lat_g": np.concatenate([feature_columns(x["q_norm_g_2"]), feature_columns(x["kv_norm_g_2"])], axis=1),
        "ffn_conv_w": np.concatenate([taps_last(x["ffn_conv_w_2"][i]) for i in range(2)], axis=1),
    }
    arrays = {
        "params": np.ascontiguousarray(np.concatenate([packed[name] for name, _ in PARAM_WIDTHS], axis=1)),
        "x_t": np.ascontiguousarray(x["x"][0].T), "p_t": np.ascontiguousarray(x["p"][:, 0].transpose(0, 2, 1)),
        "rel_bias": x["rel_bias"],
        "conv_w_pw1": x["conv_w_pw1"][0], "conv_w_pw2": x["conv_w_pw2"][0],
        "attn_w_qkv": x["attn_w_qkv"][0], "attn_w_o": x["attn_w_o"][0],
        "ffn_w_gate": x["ffn_w_gate"], "ffn_w_up": x["ffn_w_up"], "ffn_w_down": x["ffn_w_down"],
        "ple_w_gate": x["ple_w_gate"], "ple_w_proj": x["ple_w_proj"],
        "ada_w": x["ada_w_2"], "ev_w_in": x["ev_w_in_2"][0], "ev_w_out": x["ev_w_out_2"][0],
        "od_w_in": x["od_w_in_2"][0], "pool_w": x["pool_w_2"][0], "w_uq": x["w_uq_2"][0],
        "w_ukv": x["w_ukv_2"][0], "od_w_out": x["od_w_out_2"][0],
        "ffn_w_up2": x["ffn_w_up_2"], "ffn_w_down2": x["ffn_w_down_2"],
        **constant_arrays(),
    }
    nc = bacc.Bacc("TRN2", target_bir_lowering=False, num_devices=1)
    feeds, aps = {}, {}
    for name, v in arrays.items():
        feeds[f"in_{name}"] = np.ascontiguousarray(v)
        aps[name] = nc.dram_tensor(f"in_{name}", v.shape, F32, kind="ExternalInput").ap()
    out = nc.dram_tensor("out_t", (D, S), F32, kind="ExternalOutput").ap()
    build(nc, aps, out)
    result = run_bass_kernel_spmd(nc, [feeds], core_ids=[0])
    return np.ascontiguousarray(result.results[0]["out_t"].T)[None]
```
